# Optimizing a Trainium2 kernel written in Bass

```python
import math
import jax
import jax.numpy as jnp
from jax import lax
import numpy as np

D_MODEL = 1024
BATCH = 1
SEQ = 256
DEPTH = 2

GRID_W = 64
CTX_LEN = 256
HEAD_DIM = 64
ATTN_SCALE = HEAD_DIM ** -0.5
BLOCK = 128
N_MIX_HEADS = D_MODEL // HEAD_DIM
A_HEADS = N_MIX_HEADS // 2
A_KV_HEADS = A_HEADS // 4
A_WINDOW = 128
B_HEADS = N_MIX_HEADS - A_HEADS
NA_KH_MAX = 8
NA_KW = 16
NA_QCOLS = 16
NA_KCOLS = 32
C_HEADS = D_MODEL // (2 * HEAD_DIM)
C_VDIM = 2 * HEAD_DIM
ROPE_THETA = 10000.0
ROPE_AXIS_DIM = HEAD_DIM // 2
FF_DIM = 256 * math.ceil(8 * D_MODEL / (3 * 256))
N_EXPERTS = 8
TOP_K = 2
EXPERT_FF = 7 * D_MODEL // 2
LN_EPS = 1e-5
N_EVEN = (DEPTH + 1) // 2
N_ODD = DEPTH // 2
DN_ALPHA = (2 * DEPTH) ** 0.25
DN_BETA = (8 * DEPTH) ** -0.25
MASK_VALUE = -1e30
A_Q = A_HEADS * HEAD_DIM
A_KV = A_KV_HEADS * HEAD_DIM
B_W = B_HEADS * HEAD_DIM
AB_SPLITS = [A_Q, A_Q + A_KV, A_Q + 2 * A_KV, A_Q + 2 * A_KV + B_W, A_Q + 2 * A_KV + 2 * B_W]
AB_IN = A_Q + 2 * A_KV + 3 * B_W
AB_OUT = A_Q + B_W
C_QK = C_HEADS * 2 * HEAD_DIM
C_OUT = C_HEADS * C_VDIM
C_IN = 2 * C_QK + C_OUT

kernel_name = 'hybrid_diffusion_trunk'

def _layernorm(x, g, b):
    xf = x.astype(jnp.float32)
    mu = jnp.mean(xf, axis=-1, keepdims=True)
    var = jnp.mean(jnp.square(xf - mu), axis=-1, keepdims=True)
    y = (xf - mu) * lax.rsqrt(var + LN_EPS) * g.astype(jnp.float32) + b.astype(jnp.float32)
    return y.astype(x.dtype)

def _rms_norm(x, g):
    xf = x.astype(jnp.float32)
    y = xf * lax.rsqrt(jnp.mean(jnp.square(xf), axis=-1, keepdims=True) + LN_EPS) * g.astype(jnp.float32)
    return y.astype(x.dtype)

def _rope_tables(n):
    t = jnp.arange(n, dtype=jnp.int32)
    row = (t // GRID_W).astype(jnp.float32)
    col = (t % GRID_W).astype(jnp.float32)
    inv = ROPE_THETA ** (-jnp.arange(0, ROPE_AXIS_DIM, 2, dtype=jnp.float32) / ROPE_AXIS_DIM)
    ar = row[:, None] * inv[None, :]
    ac = col[:, None] * inv[None, :]
    ang = jnp.concatenate([ar, ar, ac, ac], axis=-1)
    return jnp.cos(ang), jnp.sin(ang)

def _rope2d(x, cos, sin):
    x1, x2, x3, x4 = jnp.split(x, 4, axis=-1)
    rot = jnp.concatenate([-x2, x1, -x4, x3], axis=-1)
    shape = (1, cos.shape[0]) + (1,) * (x.ndim - 3) + (HEAD_DIM,)
    return (x * cos.reshape(shape) + rot * sin.reshape(shape)).astype(x.dtype)

def _window_gqa(q, k, v, kc, vc, sink):
    B, N, HA, Dh = q.shape
    KV = k.shape[2]
    G = HA // KV
    NB = N // BLOCK
    C = kc.shape[1]
    L = 3 * BLOCK
    qb = q.reshape(B, NB, BLOCK, KV, G, Dh)

    def band(t):
        tp = jnp.pad(t, ((0, 0), (BLOCK, BLOCK), (0, 0), (0, 0))).reshape(B, NB + 2, BLOCK, KV, Dh)
        return jnp.concatenate([tp[:, :-2], tp[:, 1:-1], tp[:, 2:]], axis=2)

    kb, vb = band(k), band(v)
    s_loc = jnp.einsum('bnqkgd,bnskd->bnkgqs', qb, kb, preferred_element_type=jnp.float32) * ATTN_SCALE
    qi = jnp.arange(BLOCK)[:, None]
    si = jnp.arange(L)[None, :]
    kpos = jnp.arange(NB)[:, None, None] * BLOCK - BLOCK + si[None]
    valid = (jnp.abs(si - BLOCK - qi) <= A_WINDOW)[None] & (kpos >= 0) & (kpos < N)
    s_loc = jnp.where(valid[None, :, None, None], s_loc, MASK_VALUE)
    s_ctx = jnp.einsum('bnqkgd,bckd->bnkgqc', qb, kc, preferred_element_type=jnp.float32) * ATTN_SCALE
    s_sink = jnp.broadcast_to(sink.reshape(KV, G, 1, 1).astype(jnp.float32), s_loc.shape[:-1] + (1,))
    p = jax.nn.softmax(jnp.concatenate([s_loc, s_ctx, s_sink], axis=-1), axis=-1).astype(v.dtype)
    o = (jnp.einsum('bnkgqs,bnskd->bnqkgd', p[..., :L], vb)
         + jnp.einsum('bnkgqc,bckd->bnqkgd', p[..., L:L + C], vc))
    return o.reshape(B, N, HA, Dh)

def _ctx_gqa(q, k, v, sink):
    B, C, HA, Dh = q.shape
    KV = k.shape[2]
    G = HA // KV
    qg = q.reshape(B, C, KV, G, Dh)
    s = jnp.einsum('bqkgd,bskd->bkgqs', qg, k, preferred_element_type=jnp.float32) * ATTN_SCALE
    s_sink = jnp.broadcast_to(sink.reshape(KV, G, 1, 1).astype(jnp.float32), s.shape[:-1] + (1,))
    p = jax.nn.softmax(jnp.concatenate([s, s_sink], axis=-1), axis=-1)[..., :C].astype(v.dtype)
    return jnp.einsum('bkgqs,bskd->bqkgd', p, v).reshape(B, C, HA, Dh)

def _ctx_mha(q, k, v):
    s = jnp.einsum('bqhd,bshd->bhqs', q, k, preferred_element_type=jnp.float32) * ATTN_SCALE
    p = jax.nn.softmax(s, axis=-1).astype(v.dtype)
    return jnp.einsum('bhqs,bshd->bqhd', p, v)

def _neighbourhood_attn(q, k, v, kc, vc, rpb, rows):
    B, N, H, Dh = q.shape
    KH = min(NA_KH_MAX, rows)
    NCB = GRID_W // NA_QCOLS
    S = KH * NA_KCOLS
    r = jnp.arange(rows)
    rs = jnp.clip(r - KH // 2, 0, rows - KH)
    key_rows = rs[:, None] + jnp.arange(KH)[None, :]
    qcols = jnp.arange(GRID_W).reshape(NCB, NA_QCOLS)
    kc0 = jnp.clip(jnp.arange(NCB) * NA_QCOLS - NA_KW // 2, 0, GRID_W - NA_KCOLS)
    key_cols = kc0[:, None] + jnp.arange(NA_KCOLS)[None, :]
    idx = (key_rows[:, None, :, None] * GRID_W + key_cols[None, :, None, :]).reshape(rows, NCB, S)
    kg = k[:, idx]
    vg = v[:, idx]
    qb = q.reshape(B, rows, NCB, NA_QCOLS, H, Dh)
    s = jnp.einsum('brjqhd,brjshd->brjhqs', qb, kg, preferred_element_type=jnp.float32) * ATTN_SCALE
    cs = jnp.clip(qcols - NA_KW // 2, 0, GRID_W - NA_KW)
    col_ok = (key_cols[:, None, :] >= cs[:, :, None]) & (key_cols[:, None, :] < cs[:, :, None] + NA_KW)
    mask = jnp.broadcast_to(col_ok[:, :, None, :], (NCB, NA_QCOLS, KH, NA_KCOLS)).reshape(NCB, NA_QCOLS, S)
    dr = key_rows - r[:, None]
    dc = key_cols[:, None, :] - qcols[:, :, None]
    dr_i = dr + NA_KH_MAX - 1
    dc_i = jnp.clip(dc + NA_KW - 1, 0, 2 * NA_KW - 2)
    bias = rpb[:, dr_i[:, None, None, :, None], dc_i[None, :, :, None, :]]
    bias = jnp.transpose(bias, (1, 2, 0, 3, 4, 5)).reshape(rows, NCB, H, NA_QCOLS, S).astype(jnp.float32)
    s = jnp.where(mask[None, None, :, None], s + bias[None], MASK_VALUE)
    s_ctx = jnp.einsum('brjqhd,bchd->brjhqc', qb, kc, preferred_element_type=jnp.float32) * ATTN_SCALE
    p = jax.nn.softmax(jnp.concatenate([s, s_ctx], axis=-1), axis=-1).astype(v.dtype)
    o = (jnp.einsum('brjhqs,brjshd->brjqhd', p[..., :S], vg)
         + jnp.einsum('brjhqc,bchd->brjqhd', p[..., S:], vc))
    return o.reshape(B, N, H, Dh)

def _mixer_ab(hx, hc, w_in, w_out, sink, rpb, cos, sin, with_ctx):
    B, N, _ = hx.shape
    rows = N // GRID_W

    def proj(h):
        T = h.shape[1]
        qa, ka, va, qb, kb, vb = jnp.split(h @ w_in, AB_SPLITS, axis=-1)
        return (qa.reshape(B, T, A_HEADS, HEAD_DIM), ka.reshape(B, T, A_KV_HEADS, HEAD_DIM),
                va.reshape(B, T, A_KV_HEADS, HEAD_DIM), qb.reshape(B, T, B_HEADS, HEAD_DIM),
                kb.reshape(B, T, B_HEADS, HEAD_DIM), vb.reshape(B, T, B_HEADS, HEAD_DIM))

    qa, ka, va, qb, kb, vb = proj(hx)
    qa_c, ka_c, va_c, qb_c, kb_c, vb_c = proj(hc)
    qa = _rope2d(qa, cos, sin)
    ka = _rope2d(ka, cos, sin)
    oa = _window_gqa(qa, ka, va, ka_c, va_c, sink)
    ob = _neighbourhood_attn(qb, kb, vb, kb_c, vb_c, rpb, rows)
    yx = jnp.concatenate([oa.reshape(B, N, A_Q), ob.reshape(B, N, B_W)], axis=-1) @ w_out
    if not with_ctx:
        return yx, None
    C = hc.shape[1]
    oa_c = _ctx_gqa(qa_c, ka_c, va_c, sink)
    ob_c = _ctx_mha(qb_c, kb_c, vb_c)
    yc = jnp.concatenate([oa_c.reshape(B, C, A_Q), ob_c.reshape(B, C, B_W)], axis=-1) @ w_out
    return yx, yc

def _diff_attn_block(q, k_all, v_all, lam):
    s = jnp.einsum('bqhid,bshid->bhiqs', q, k_all, preferred_element_type=jnp.float32) * ATTN_SCALE
    p = jax.nn.softmax(s, axis=-1)
    a = (p[:, :, 0] - lam * p[:, :, 1]).astype(v_all.dtype)
    return jnp.einsum('bhqs,bshe->bqhe', a, v_all)

def _mixer_c(hx, hc, w_in, w_out, lam_p, subln, lam_init, cos, sin, with_ctx):
    B, N, _ = hx.shape
    C = hc.shape[1]
    lp = lam_p.astype(jnp.float32)
    lam = jnp.exp(jnp.sum(lp[0] * lp[1])) - jnp.exp(jnp.sum(lp[2] * lp[3])) + lam_init

    def proj(h):
        T = h.shape[1]
        q, k, v = jnp.split(h @ w_in, [C_QK, 2 * C_QK], axis=-1)
        return (q.reshape(B, T, C_HEADS, 2, HEAD_DIM), k.reshape(B, T, C_HEADS, 2, HEAD_DIM),
                v.reshape(B, T, C_HEADS, C_VDIM))

    def finish(o, T):
        o = _rms_norm(o, subln) * (1.0 - lam_init)
        return o.reshape(B, T, C_OUT) @ w_out

    qx, kx, vx = proj(hx)
    qc, kc, vc = proj(hc)
    qx = _rope2d(qx, cos, sin)
    kx = _rope2d(kx, cos, sin)
    k_all = jnp.concatenate([kx, kc], axis=1)
    v_all = jnp.concatenate([vx, vc], axis=1)
    NB = N // BLOCK
    qblocks = jnp.moveaxis(qx.reshape(B, NB, BLOCK, C_HEADS, 2, HEAD_DIM), 1, 0)

    def one_block(qb):
        return _diff_attn_block(qb, k_all, v_all, lam)

    o = lax.map(one_block, qblocks)
    o = jnp.moveaxis(o, 0, 1).reshape(B, N, C_HEADS, C_VDIM)
    yx = finish(o, N)
    if not with_ctx:
        return yx, None
    yc = finish(_diff_attn_block(qc, kc, vc, lam), C)
    return yx, yc

def _swiglu(h, w_up, w_down):
    g, u = jnp.split(h @ w_up, 2, axis=-1)
    return (jax.nn.silu(g) * u) @ w_down

def _moe(h, w_router, w_up, w_down):
    B, T, D = h.shape
    hf = h.reshape(B * T, D)
    logits = (hf @ w_router).astype(jnp.float32)
    top_val, top_idx = lax.top_k(logits, TOP_K)
    top_w = jax.nn.softmax(top_val, axis=-1)
    gates = jnp.sum(jax.nn.one_hot(top_idx, N_EXPERTS, dtype=jnp.float32) * top_w[..., None], axis=1)
    gates = gates.astype(h.dtype)
    out = jnp.zeros_like(hf)
    for e in range(N_EXPERTS):
        out = out + gates[:, e:e + 1] * _swiglu(hf, w_up[e], w_down[e])
    return out.reshape(B, T, D)

def _lambda_init(layer):
    return 0.8 - 0.6 * math.exp(-0.3 * layer)

def setup_inputs(seed: int = 0) -> dict:
    key = jax.random.key(seed)
    ks = jax.random.split(key, 32)
    f32 = jnp.float32
    D = D_MODEL

    def nrm(i, shape, scale):
        return jax.random.normal(ks[i], shape, f32) * scale

    sd = D ** -0.5
    x = nrm(0, (BATCH, SEQ, D), 1.0)
    c = nrm(1, (BATCH, D), 1.0)
    ctx = nrm(2, (BATCH, CTX_LEN, D), 1.0)
    c_ctx = nrm(3, (D,), 1.0)
    w_mod = nrm(4, (DEPTH, D, 6 * D), 0.5 * sd)
    b_mod = nrm(5, (DEPTH, 6 * D), 0.02)
    ln_g = 1.0 + nrm(6, (DEPTH, 2, D), 0.02)
    ln_b = nrm(7, (DEPTH, 2, D), 0.02)
    w_in_ab = jnp.concatenate([
        nrm(8, (N_EVEN, D, A_Q + A_KV), sd),
        nrm(9, (N_EVEN, D, A_KV), sd * DN_BETA),
        nrm(10, (N_EVEN, D, 2 * B_W), sd),
        nrm(11, (N_EVEN, D, B_W), sd * DN_BETA),
    ], axis=-1)
    w_out_ab = nrm(12, (N_EVEN, AB_OUT, D), AB_OUT ** -0.5 * DN_BETA)
    sink_a = nrm(13, (N_EVEN, A_HEADS), 1.0)
    rpb_b = nrm(14, (N_EVEN, B_HEADS, 2 * NA_KH_MAX - 1, 2 * NA_KW - 1), 0.1)
    w_in_c = jnp.concatenate([
        nrm(15, (N_ODD, D, 2 * C_QK), sd),
        nrm(16, (N_ODD, D, C_OUT), sd * DN_BETA),
    ], axis=-1)
    w_out_c = nrm(17, (N_ODD, C_OUT, D), C_OUT ** -0.5 * DN_BETA)
    lam_c = nrm(18, (N_ODD, 4, HEAD_DIM), 0.1)
    subln_c = 1.0 + nrm(19, (N_ODD, C_VDIM), 0.02)
    w_ffn_up = nrm(20, (N_EVEN, D, 2 * FF_DIM), sd)
    w_ffn_down = nrm(21, (N_EVEN, FF_DIM, D), FF_DIM ** -0.5 * DN_BETA)
    w_router = nrm(22, (N_ODD, D, N_EXPERTS), sd)
    w_exp_up = nrm(23, (N_ODD, N_EXPERTS, D, 2 * EXPERT_FF), sd)
    w_exp_down = nrm(24, (N_ODD, N_EXPERTS, EXPERT_FF, D), EXPERT_FF ** -0.5 * DN_BETA)
    return {'x': x, 'c': c, 'ctx': ctx, 'c_ctx': c_ctx, 'w_mod': w_mod, 'b_mod': b_mod,
            'ln_g': ln_g, 'ln_b': ln_b, 'w_in_ab': w_in_ab, 'w_out_ab': w_out_ab, 'sink_a': sink_a,
            'rpb_b': rpb_b, 'w_in_c': w_in_c, 'w_out_c': w_out_c, 'lam_c': lam_c, 'subln_c': subln_c,
            'w_ffn_up': w_ffn_up, 'w_ffn_down': w_ffn_down, 'w_router': w_router,
            'w_exp_up': w_exp_up, 'w_exp_down': w_exp_down}

def reference(x, c, ctx, c_ctx, w_mod, b_mod, ln_g, ln_b, w_in_ab, w_out_ab, sink_a, rpb_b,
              w_in_c, w_out_c, lam_c, subln_c, w_ffn_up, w_ffn_down, w_router, w_exp_up, w_exp_down):
    B, N, D = x.shape
    C = ctx.shape[1]
    cos, sin = _rope_tables(N)
    sc = jax.nn.silu(c)
    scc = jax.nn.silu(c_ctx)
    for l in range(DEPTH):
        last = l == DEPTH - 1
        i = l // 2
        mod_x = (sc @ w_mod[l] + b_mod[l])[:, None, :]
        mod_c = (scc @ w_mod[l] + b_mod[l])[None, None, :]
        shx1, scx1, gx1, shx2, scx2, gx2 = jnp.split(mod_x, 6, axis=-1)
        shc1, scc1, gc1, shc2, scc2, gc2 = jnp.split(mod_c, 6, axis=-1)
        hx = x * (1.0 + scx1) + shx1
        hc = ctx * (1.0 + scc1) + shc1
        if l % 2 == 0:
            yx, yc = _mixer_ab(hx, hc, w_in_ab[i], w_out_ab[i], sink_a[i], rpb_b[i], cos, sin, not last)
        else:
            yx, yc = _mixer_c(hx, hc, w_in_c[i], w_out_c[i], lam_c[i], subln_c[i], _lambda_init(l),
                              cos, sin, not last)
        x = _layernorm(DN_ALPHA * x + gx1 * yx, ln_g[l, 0], ln_b[l, 0])
        if l % 2 == 0:
            ffn = functools_free_ffn = (lambda h, _i=i: _swiglu(h, w_ffn_up[_i], w_ffn_down[_i]))
        else:
            ffn = (lambda h, _i=i: _moe(h, w_router[_i], w_exp_up[_i], w_exp_down[_i]))
        if not last:
            ctx = _layernorm(DN_ALPHA * ctx + gc1 * yc, ln_g[l, 0], ln_b[l, 0])
            h = jnp.concatenate([ctx * (1.0 + scc2) + shc2, x * (1.0 + scx2) + shx2], axis=1)
            f = ffn(h)
            ctx = _layernorm(DN_ALPHA * ctx + gc2 * f[:, :C], ln_g[l, 1], ln_b[l, 1])
            x = _layernorm(DN_ALPHA * x + gx2 * f[:, C:], ln_g[l, 1], ln_b[l, 1])
        else:
            f = ffn(x * (1.0 + scx2) + shx2)
            x = _layernorm(DN_ALPHA * x + gx2 * f, ln_g[l, 1], ln_b[l, 1])
    return x


_drawn_inputs = setup_inputs


def setup_inputs(seed=0):
    import zlib

    import numpy as np

    out = dict(_drawn_inputs(seed))
    spreads = {}
    factors = {'b_mod': 4.75,
     'w_in_ab': 2.885,
     'w_out_ab': 3.748,
     'sink_a': 64.0,
     'rpb_b': 8.0,
     'lam_c': 3.185,
     'subln_c': 45.409}
    for name, (base, spread) in spreads.items():
        noise = np.random.default_rng([zlib.crc32(name.encode()), seed]).standard_normal(out[name].shape)
        drawn = base * np.exp(spread * noise) if base else spread * noise
        out[name] = jnp.asarray(drawn.astype(out[name].dtype))
    for name, factor in factors.items():
        out[name] = (out[name] * factor).astype(out[name].dtype)
    return out
```

```python
import math
from contextlib import ExitStack

import numpy as np

import concourse.bass as bass
from concourse import mybir

F32 = mybir.dt.float32
F32R = mybir.dt.float32r
U32 = mybir.dt.uint32
ALU = mybir.AluOpType
ACT = mybir.ActivationFunctionType
AX = mybir.AxisListType

P = 128
D = 1024
KT = D // P
SEQ = 256
CTX = 256
BLK = 4
TOK = BLK * P
DEPTH = 2
HD = 64
GRID_W = 64
ROWS = SEQ // GRID_W
A_HEADS = 8
A_KV = 2
B_HEADS = 8
C_HEADS = 8
KH_MAX = 8
NKW = 16
WINDOW = 128
FF = 2816
FT = FF // P
NE = 8
EFF = 3584
EFT = EFF // P
EPS = 1e-5
ALPHA = (2 * DEPTH) ** 0.25
SCALE = HD ** -0.5
MASK = -1e30 / SCALE
LAM_INIT = 0.8 - 0.6 * math.exp(-0.3)

CW = 2048
NB_MOD = 6 * D // 512
N_MOD = DEPTH * NB_MOD * 2
RING = 4
MRING = 7
DR = 2 * KH_MAX - 1
DC = 2 * NKW - 1
ZL = 2 * GRID_W - 1

C_ID, C_ROT, C_MA, C_MB, C_COS, C_SIN, C_IOTA = 0, 128, 256, 768, 832, 1088, 1344
C_ALL = 1352


def shape_constants():
    cn = np.zeros((P, C_ALL), np.float32)
    cn[:, C_ID:C_ID + P] = np.eye(P, dtype=np.float32)
    rot = np.zeros((P, P), np.float32)
    for m in range(P):
        q = (m % 64) // 16
        if q % 2 == 0:
            rot[m, m + 16] = -1.0
        else:
            rot[m, m - 16] = 1.0
    cn[:, C_ROT:C_ROT + P] = rot.T
    for b in range(2):
        qi = b * P + np.arange(P)[:, None]
        ki = np.arange(SEQ)[None, :]
        cn[:, C_MA + b * SEQ:C_MA + (b + 1) * SEQ] = np.where(np.abs(qi - ki) <= WINDOW, 0.0, MASK)
    col = (np.arange(P) % GRID_W)[:, None]
    start = np.clip(col - NKW // 2, 0, GRID_W - NKW)
    kc = np.arange(GRID_W)[None, :]
    cn[:, C_MB:C_MB + GRID_W] = np.where((kc >= start) & (kc < start + NKW), 0.0, MASK)
    t = np.arange(SEQ)
    half = HD // 2
    inv = np.float32(10000.0) ** (-np.arange(0, half, 2, dtype=np.float32) / np.float32(half))
    ar = (t // GRID_W).astype(np.float32)[:, None] * inv
    ac = (t % GRID_W).astype(np.float32)[:, None] * inv
    ang = np.concatenate([ar, ar, ac, ac], -1).astype(np.float32)
    ang = np.concatenate([ang, ang], -1).T
    cn[:, C_COS:C_COS + SEQ] = np.cos(ang)
    cn[:, C_SIN:C_SIN + SEQ] = np.sin(ang)
    cn[:, C_IOTA:C_IOTA + 8] = np.arange(8, dtype=np.float32)
    return cn


def trunk(nc, x, ctx_in, vecs, consts, w_mod, ln_g, ln_b, w_in_ab, w_out_ab, sink_a, rpb, w_in_c,
          w_out_c, lam_c, subln, w_up, w_down, w_router, w_eup, w_edown, out):
    ctx = ExitStack()
    with ctx:
        base = 16512

        def sb(name, shape, dt, off):
            return nc.alloc_sbuf_tensor_at(name, shape, dt, offset=base + off)

        def sem(name):
            return ctx.enter_context(nc.semaphore(name))

        K = 1024
        X = sb("X", [P, BLK, D], F32, 0)
        HH = sb("HH", [P, KT, TOK], F32R, 16 * K)
        HL = sb("HL", [P, KT, TOK], F32R, 32 * K)
        RAW = sb("RAW", [P, RING, CW], F32, 48 * K)
        WH = sb("WH", [P, 2, CW], F32R, 80 * K)
        WL = sb("WL", [P, 2, CW], F32R, 96 * K)
        CN = sb("CN", [P, C_ALL], F32, 112 * K)
        o = 112 * K + 5440
        ZERO = sb("ZERO", [P, 512], F32, o); o += 2048
        VT = sb("VT", [P, 112], F32, o); o += 448
        ST = sb("ST", [P, KT, 2], F32, o); o += 64
        MODC = sb("MODC", [P, DEPTH, 48, 2], F32, o); o += 768
        SINK = sb("SINK", [P, A_HEADS], F32, o); o += 32
        LAMP = sb("LAMP", [P, 4 * HD], F32, o); o += 1024
        SUBL = sb("SUBL", [P, P], F32, o); o += 512
        SM = sb("SM", [P, 512], F32, o); o += 2048
        IDX = sb("IDX", [P, 8], U32, o); o += 32
        R0 = 125 * K
        assert o <= R0, o
        F = sb("F", [P, KT, TOK], F32, R0)
        QT = sb("QT", [P, 8, TOK], F32, R0)
        KTT = sb("KTT", [P, 8, TOK], F32, R0 + 16 * K)
        V0 = sb("V0", [P, BLK, 640], F32, R0 + 32 * K)
        BIAS = sb("BIAS", [P, 2, B_HEADS, SEQ], F32, R0 + 42 * K)
        V1 = sb("V1", [P, BLK, D], F32, R0 + 32 * K)
        TQ = sb("TQ", [P, D], F32, R0 + 48 * K)
        S = sb("S", [P, 2, 4, 512], F32, R0 + 58 * K)
        PT = sb("PT", [P, 2, 512], F32, R0 + 74 * K)
        OSB = sb("OSB", [P, D], F32, R0 + 78 * K)
        ROW = sb("ROW", [2, 2, 512], F32, R0 + 58 * K)
        VR = sb("VR", [112, P], F32, R0 + 62 * K)
        ZP = sb("ZP", [B_HEADS * DR, ZL + 1], F32, R0 + 64 * K)
        GT = sb("GT", [P, FT, TOK], F32, R0)
        GH = sb("GH", [P, 2, 2, TOK], F32R, R0 + 44 * K)
        GL = sb("GL", [P, 2, 2, TOK], F32R, R0 + 52 * K)
        T = sb("T", [P, 2, 512], F32, R0 + 60 * K)
        GATE = sb("GATE", [P, 2, D], F32, R0 + 64 * K)
        LNR = sb("LNR", [P, 2, D], F32, R0 + 72 * K)
        TMP = sb("TMP", [P, 512], F32, R0 + 80 * K)
        WR = sb("WR", [P, KT, NE], F32, R0 + 81 * K + 1024)
        AF = sb("AF", [P, 2, 512], F32, R0 + 16 * K)
        AH = sb("AH", [P, 2, 512], F32R, R0 + 20 * K)
        AL = sb("AL", [P, 2, 512], F32R, R0 + 24 * K)
        ACC = sb("ACC", [P, 4, 512], F32, R0 + 28 * K)
        RAWX = sb("RAWX", [P, MRING - RING, CW], F32, R0 + 36 * K)
        MT = sb("MT", [P, 2, 512], F32, R0 + 60 * K)

        MX = lambda g: SM[:, (g % 2) * 8:(g % 2) * 8 + 8]
        MM = lambda g: SM[:, 16 + (g % 2) * 4:20 + (g % 2) * 4]
        NM = lambda g: SM[:, 24 + (g % 2) * 4:28 + (g % 2) * 4]
        SU = lambda g: SM[:, 32 + (g % 2) * 4:36 + (g % 2) * 4]
        SD = lambda g: SM[:, 40 + (g % 2) * 4:44 + (g % 2) * 4]
        SE = lambda g: SM[:, 48 + (g % 2) * 4:52 + (g % 2) * 4]
        RI = lambda g: SM[:, 56 + (g % 2) * 4:60 + (g % 2) * 4]
        LT = SM[:, 64:72]
        LAM = SM[:, 72:73]
        SS = SM[:, 80:88]
        SS2 = SM[:, 88:96]
        ST6 = SM[:, 96:144].rearrange("p (b s) -> p b s", b=4)
        MV = SM[:, 144:152].rearrange("p (b s) -> p b s", b=4)
        SV = SM[:, 152:156]
        SQ = SM[:, 156:160]
        RS = SM[:, 160:164]
        LG = SM[:, 176:184]
        M8 = SM[:, 184:192]
        EV = SM[:, 192:200]
        IF = SM[:, 200:208]
        OH = SM[:, 208:216]
        GW = SM[:, 224:240].rearrange("p (b e) -> p b e", b=2)

        PS = ctx.enter_context(nc.psum_tensor("PS", [P, 8, 512], F32))
        fbias = nc.dram_tensor("bias_rows", [B_HEADS * DR, GRID_W, ZL], F32, kind="Internal").ap()

        ident = CN[:, C_ID:C_ID + P]

        chunks = []

        def stat_chunk(w, n0):
            chunks.append(("s", w[:, n0:n0 + 256].rearrange("(k p) n -> p k n", p=P)))

        def move_chunk(w, n0, kh):
            chunks.append(("m", w[kh * 512:(kh + 1) * 512, n0:n0 + 512].rearrange("(k p) n -> p k n", p=P)))

        wi = w_in_ab[0]
        for n0 in (0, 256, 512, 768, 1024, 1280, 1536):
            stat_chunk(wi, n0)
        move_chunk(wi, 1792, 0)
        move_chunk(wi, 1792, 1)
        C_OUT0 = len(chunks)
        for nh in range(2):
            for kh in range(2):
                move_chunk(w_out_ab[0], nh * 512, kh)
        C_UP = len(chunks)
        for st in range(FT // 2):
            stat_chunk(w_up[0], st * 256)
            stat_chunk(w_up[0], FF + st * 256)
        C_DN = len(chunks)
        for j in range(FT // 2):
            chunks.append(("d", w_down[0][j * 256:(j + 1) * 256, :].rearrange("(k p) n -> p k n", p=P)))
        C_IN1 = len(chunks)
        wc = w_in_c[0]
        for i in range(8):
            stat_chunk(wc, i * 256)
        for nh in range(2):
            for kh in range(2):
                move_chunk(wc, 2048 + nh * 512, kh)
        C_OUT1 = len(chunks)
        for nh in range(2):
            for kh in range(2):
                move_chunk(w_out_c[0], nh * 512, kh)
        C_MOE = len(chunks)
        CPE = 3 * EFT // 2
        assert C_MOE % 2 == 0 and CPE % MRING == 0 and N_MOD % RING == 0

        def kview(kind, t):
            k = {"s": 8, "m": 4, "d": 2}[kind]
            return t.rearrange("p (k n) -> p k n", k=k)

        s_const = sem("constants_landed")
        s_x = sem("x_landed")
        s_small = sem("small_inputs_landed")
        s_wr = sem("router_weights_landed")
        s_landed = [sem(f"raw_landed{i}") for i in range(RING)]
        s_mland = [sem(f"expert_raw_landed{i}") for i in range(MRING)]
        s_modused = sem("mod_chunk_used")
        s_hi = sem("weights_hi_ready")
        s_lo = sem("weights_lo_ready")
        s_khalf = sem("first_contraction_half_used")
        s_vt = sem("vectors_transposed")
        s_vtc = sem("vectors_copied")
        s_silu = sem("silu_c_ready")
        s_modrow = sem("mod_row_copied")
        s_modcol = sem("mod_columns_in_psum")
        s_modc = sem("mod_columns_ready")
        s_zero = sem("zero_tile_ready")
        s_zp = sem("bias_pad_zeroed")
        s_zpl = sem("bias_pad_landed")
        s_fb = sem("bias_rows_stored")
        s_bl = sem("bias_landed")
        s_hps = sem("h_transposed")
        s_hf = sem("h_modulated")
        s_hr = sem("h_split")
        s_qps = sem("projection_in_psum")
        s_qdr = sem("projection_copied")
        s_rps = sem("rotated_in_psum")
        s_rope = sem("rope_done")
        s_sc = sem("scores_in_psum")
        s_scd = sem("scores_copied")
        s_nm = sem("negative_max_ready")
        s_sink = sem("sink_exp_done")
        s_exp = sem("exp_done")
        s_cmb = sem("difference_ready")
        s_ptp = sem("probs_transposed")
        s_ptc = sem("probs_transposed_copied")
        s_ops = sem("attention_in_psum")
        s_osb = sem("attention_copied")
        s_ob = sem("attention_block_ready")
        s_otp = sem("attention_block_transposed")
        s_oth = sem("attention_hi_ready")
        s_otr = sem("attention_split")
        s_ssq = sem("square_sums_ready")
        s_ssr = sem("square_sums_rooted")
        s_gps = sem("gate_rows_in_psum")
        s_gate = sem("gate_rows_ready")
        s_lnr = sem("norm_rows_landed")
        s_yps = sem("sublayer_out_in_psum")
        s_var = sem("variance_ready")
        s_std = sem("deviation_ready")
        s_ln = sem("norm_block_done")
        s_up = sem("up_in_psum")
        s_silg = sem("ffn_silu_done")
        s_mul = sem("ffn_product_done")
        s_gh = sem("ffn_hi_ready")
        s_gl = sem("ffn_lo_ready")
        s_dn = sem("ffn_down_chunk_done")
        s_lg = sem("router_logits_in_psum")
        s_gx = sem("router_exp_input")
        s_ge = sem("router_exp_done")
        s_mup = sem("expert_up_in_psum")
        s_msil = sem("expert_silu_done")
        s_mmul = sem("expert_product_split")
        s_mrd = sem("expert_up_banks_read")
        s_mdn = sem("expert_down_chunk_done")
        s_myd = sem("expert_out_added")
        s_out = sem("output_stored")
        s_lam = sem("lambda_exp_input")
        s_lame = sem("lambda_exp_done")
        s_dve = sem("vector_chain")

        groups = [[(b, g) for b in range(4) for g in range(4)], [(b, g) for b in (2, 3) for g in range(4)]]
        NG0 = len(groups[0])
        g_base = [0, NG0]
        pt_base = [0, 4 * NG0]
        NPT = 4 * NG0 + 2 * len(groups[1])

        def n_keys(l, b):
            return CTX if l == 0 and b < 2 else TOK

        def pts_before(gi):
            return 4 * gi if gi <= NG0 else 4 * NG0 + 2 * (gi - NG0)

        def ln_blocks(p):
            return (0, 1, 2, 3) if p < 2 else (2, 3)

        ln_before = [0, 4, 8, 10, 12]
        y_before = [0, 8, 8, 12]
        NT0 = 4 + 1 + 4 + 4 + 4 + 4
        NT1 = 8 + 8 + 8

        def head_of(l, g, j):
            if l == 1:
                return 2 * g + j // 2, j % 2, 2 * g + j // 2
            if g < 2:
                h = 4 * g + j
                return h // 2, h % 2, g
            h = 4 * (g - 2) + j
            return 4 + h // 2, h % 2, 2 + h // 2

        def values(l, g, j):
            if l == 1:
                return V1[:, :, (2 * g + j) * P:(2 * g + j + 1) * P]
            if g < 2:
                return V0[:, :, g * HD:(g + 1) * HD]
            h = 4 * (g - 2) + j
            return V0[:, :, P + h * HD:P + (h + 1) * HD]

        def rope_tiles(l):
            n = (4, 2) if l == 0 else (8, 8)
            return [(QT, j) for j in range(n[0])] + [(KTT, j) for j in range(n[1])]

        def projection(l):
            every, lat = slice(0, TOK), slice(CTX, TOK)
            plan = []
            if l == 0:
                for i in range(2):
                    plan.append([(every, QT[:, 2 * i + j, :]) for j in range(2)])
                plan.append([(every, "keys of A")] + [(slice(P, 2 * P), V0[:, b, 0:P]) for b in range(BLK)])
                for i in range(2):
                    plan.append([(every, QT[:, 4 + 2 * i + j, :]) for j in range(2)])
                for i in range(2):
                    plan.append([(every, KTT[:, 2 + 2 * i + j, :]) for j in range(2)])
                plan += [[], [(every, V0[:, b, P:P + 512]) for b in range(BLK)]]
            else:
                for i in range(4):
                    plan.append([(slice(0, SEQ), QT[:, 2 * i + j, lat]) for j in range(2)])
                for i in range(4):
                    plan.append([(every, KTT[:, 2 * i + j, :]) for j in range(2)])
                for nh in range(2):
                    plan += [[], [(every, V1[:, b, nh * 512:(nh + 1) * 512]) for b in range(BLK)]]
            c0 = 0 if l == 0 else C_IN1
            return [(c0 + i, tiles) for i, tiles in enumerate(plan)]

        used = []
        t, kh_n, y_n = 0, 0, 0
        for l in range(2):
            for c, tiles in projection(l):
                t += len(tiles)
                kh_n += not tiles
                used.append((s_qps, t) if tiles else (s_khalf, kh_n))
            for nh in range(2):
                kh_n += 1
                y_n += len(ln_blocks(2 * l))
                used += [(s_khalf, kh_n), (s_yps, y_n)]
            if l == 0:
                used += [(s_up, 2 * i + 2) for i in range(FT)]
                used += [(s_dn, j + 1) for j in range(FT // 2)]
        assert len(used) == C_MOE and t == NT0 + NT1

        block = ctx.enter_context(nc.Block())

        def expert_chunk(q):
            order = [("g", 0), ("u", 0)]
            for st in range(1, EFT // 2):
                order += [("g", st), ("u", st), ("d", st - 1)]
            order.append(("d", EFT // 2 - 1))
            return order[q]

        @block.sync
        def _(sp):
            sp.dma_start(VR[:, :], vecs).then_inc(s_const, 16)
            sp.dma_start(CN[:, :], consts).then_inc(s_const, 16)
            wm = w_mod.rearrange("l (kh k p) n -> l kh p k n", kh=2, p=P)
            for c in range(N_MOD):
                if c >= RING:
                    sp.wait_ge(s_modused, c - RING + 1)
                l, nb, kh = c // (2 * NB_MOD), c // 2 % NB_MOD, c % 2
                sp.dma_start(kview("m", RAW[:, c % RING, :]),
                             wm[l, kh][:, :, nb * 512:(nb + 1) * 512]).then_inc(s_landed[c % RING], 16)
            for c, (kind, src) in enumerate(chunks):
                if c < RING:
                    sp.wait_ge(s_modused, N_MOD - RING + c + 1)
                else:
                    sp.wait_ge(s_lo, c - RING + 1)
                sp.dma_start(kview(kind, RAW[:, c % RING, :]), src).then_inc(s_landed[c % RING], 16)
            sp.wait_ge(s_lo, C_MOE)
            up = w_eup[0].rearrange("e (k p) n -> p e k n", p=P)
            dn = w_edown[0].rearrange("e (k p) n -> p e k n", p=P)
            with sp.Fori(0, NE) as e:
                for q in range(CPE):
                    slot = q % MRING
                    dst = RAW[:, slot, :] if slot < RING else RAWX[:, slot - RING, :]
                    sp.wait_ge(s_lo, e * CPE + (C_MOE - MRING + q + 1))
                    what, st = expert_chunk(q)
                    if what == "d":
                        sp.dma_start(kview("d", dst), dn[:, bass.ds(e, 1), st * 2:st * 2 + 2, :]
                                     .rearrange("p e k n -> p (e k) n")).then_inc(s_mland[slot], 16)
                    else:
                        n0 = st * 256 + (EFF if what == "u" else 0)
                        sp.dma_start(kview("s", dst), up[:, bass.ds(e, 1), :, n0:n0 + 256]
                                     .rearrange("p e k n -> p (e k) n")).then_inc(s_mland[slot], 16)
            for b in (2, 3):
                sp.wait_ge(s_ln, ln_before[3] + b - 1)
                sp.dma_start(out[0, (b - 2) * P:(b - 1) * P, :], X[:, b, :]).then_inc(s_out, 16)
            sp.wait_ge(s_out, 32)

        @block.gpsimd
        def _(gp):
            gp.memset(ZP[:, :], 0.0).then_inc(s_zp, 1)
            gp.memset(ZERO[:, :], 0.0).then_inc(s_zero, 1)
            for b in range(2):
                gp.dma_start(X[:, b, :], ctx_in[0, b * P:(b + 1) * P, :]).then_inc(s_x, 16)
                gp.dma_start(X[:, 2 + b, :], x[0, b * P:(b + 1) * P, :]).then_inc(s_x, 16)
            gp.dma_start(SINK[:, :], sink_a[0].partition_broadcast(P)).then_inc(s_small, 16)
            gp.dma_start(LAMP[:, :], lam_c[0].rearrange("a b -> (a b)").partition_broadcast(P)).then_inc(s_small, 16)
            gp.dma_start(SUBL[:, :], subln[0].partition_broadcast(P)).then_inc(s_small, 16)
            gp.wait_ge(s_zp, 1)
            gp.dma_start(ZP[:, GRID_W - NKW:GRID_W - NKW + DC],
                         rpb[0].rearrange("h r c -> (h r) c")).then_inc(s_zpl, 16)
            gp.wait_ge(s_zpl, 16)
            rows = ZP[:, 0:ZL]
            gp.dma_start(fbias, rows.unsqueeze(1).to_broadcast([B_HEADS * DR, GRID_W, ZL])).then_inc(s_fb, 16)
            gp.wait_ge(s_fb, 16)
            fb = fbias.rearrange("(h r) c z -> r h (c z)", h=B_HEADS)
            for r in range(ROWS):
                for kr in range(ROWS):
                    src = fb[kr - r + KH_MAX - 1][:, GRID_W - 1:GRID_W - 1 + GRID_W * (ZL - 1)]
                    src = src.rearrange("h (c y) -> c h y", y=ZL - 1)[:, :, 0:GRID_W]
                    p0 = (r % 2) * GRID_W
                    gp.dma_start(BIAS[p0:p0 + GRID_W, r // 2, :, kr * GRID_W:(kr + 1) * GRID_W], src)\
                        .then_inc(s_bl, 16)
            for p in range(4):
                if p % 2 == 0:
                    gp.wait_ge(s_otr, 4 if p == 0 else 6)
                else:
                    gp.wait_ge(s_ln, ln_before[p])
                gp.dma_start(LNR[:, 0, :], ln_g[p // 2, p % 2].partition_broadcast(P)).then_inc(s_lnr, 16)
                gp.dma_start(LNR[:, 1, :], ln_b[p // 2, p % 2].partition_broadcast(P)).then_inc(s_lnr, 16)
                if p == 2:
                    gp.dma_start(WR[:, :, :], w_router[0].rearrange("(k p) e -> p k e", p=P)).then_inc(s_wr, 16)

        @block.tensor
        def _(pe):
            mm = nc.tensor.matmul

            def mm3(ps, ah, al, bh, bl, start, stop):
                mm(ps, ah, bh, start=start, stop=False)
                mm(ps, ah, bl, start=False, stop=False)
                return mm(ps, al, bh, start=False, stop=stop)

            pe.wait_ge(s_const, 32)
            nc.tensor.transpose(PS[:, 7, 0:112], VR[:, :], CN[0:112, C_ID:C_ID + 112]).then_inc(s_vt, 1)

            def mod_columns(n):
                pe.wait_ge(s_modrow, n + 1)
                l, nb = divmod(n, NB_MOD)
                for j in range(4):
                    last = mm(PS[:, 2 + l, (nb * 4 + j) * 2:(nb * 4 + j) * 2 + 2],
                              ROW[:, n % 2, j * P:(j + 1) * P], CN[0:2, C_ID:C_ID + 2], start=True, stop=True)
                if nb == NB_MOD - 1:
                    last.then_inc(s_modcol, 1)

            pe.wait_ge(s_silu, 2)
            for n in range(DEPTH * NB_MOD):
                if n >= 2:
                    pe.wait_ge(s_modrow, n - 1)
                for kh in range(2):
                    c = 2 * n + kh
                    pe.wait_ge(s_landed[c % RING], 16 * (c // RING + 1))
                    w = kview("m", RAW[:, c % RING, :])
                    for k in range(4):
                        last = mm(PS[0:2, n % 2, :], ST[:, kh * 4 + k, :], w[:, k, :],
                                  start=(kh == 0 and k == 0), stop=(kh == 1 and k == 3))
                    last.then_inc(s_modused, 1)
                if n >= 1:
                    mod_columns(n - 1)
            mod_columns(DEPTH * NB_MOD - 1)

            def h_phase(h):
                bs = ln_blocks(h) if h == 3 else (0, 1, 2, 3)
                if h == 0:
                    pe.wait_ge(s_x, 64)
                    pe.wait_ge(s_modc, 2)
                else:
                    pe.wait_ge(s_ln, ln_before[h])
                for dt in range(KT):
                    if dt >= 4:
                        pe.wait_ge(s_hf, 8 * h + dt - 3)
                    for b in bs:
                        last = nc.tensor.transpose(PS[:, dt % 4, b * P:(b + 1) * P],
                                                   X[:, b, dt * P:(dt + 1) * P], ident)
                    last.then_inc(s_hps, 1)

            def gates(p):
                l, seg = p // 2, 2 if p % 2 == 0 else 5
                for s, st in ((0, 1), (1, 0)) if l == 0 else ((1, 0),):
                    for half in range(2):
                        for j in range(4):
                            col = MODC[:, l, seg * 8 + half * 4 + j, st:st + 1].to_broadcast([P, P])
                            last = mm(PS[:, 4 + s * 2 + half, j * P:(j + 1) * P], col, ident,
                                      start=True, stop=True)
                        last.then_inc(s_gps, 1)

            def split_ready(c):
                pe.wait_ge(s_lo, c + 1)
                return c % 2

            def project(l):
                t0 = 0 if l == 0 else NT0
                c = 0 if l == 0 else C_IN1
                t = [t0]
                pe.wait_ge(s_hr, 8 * (2 * l + 1))

                def tile(n, fill):
                    if t[0] - t0 >= 8:
                        pe.wait_ge(s_qdr, t[0] - 7)
                    fill(PS[:, t[0] % 8, 0:n]).then_inc(s_qps, 1)
                    t[0] += 1

                def standing(w, lo, cols, toks):
                    def fill(ps):
                        for k in range(KT):
                            last = mm3(ps, cols(WH, w, k), cols(WL, w, k), HH[:, k, toks], HL[:, k, toks],
                                       k == 0, k == KT - 1)
                        return last
                    return fill

                def plain(n0):
                    return lambda W, w, k: kview("s", W[:, w, :])[:, k, n0:n0 + P]

                every, lat = slice(0, TOK), slice(CTX, TOK)
                if l == 0:
                    plan = ["q", "q", "a", "q", "q", "k", "k"]
                else:
                    plan = ["q"] * 4 + ["k"] * 4
                for kind in plan:
                    w = split_ready(c)
                    if kind == "a":
                        tile(TOK, standing(w, 0, plain(0), every))
                        for b in range(BLK):
                            def fill(ps, b=b):
                                for k in range(KT):
                                    tk = slice(b * P, (b + 1) * P)
                                    last = mm3(ps, HH[:, k, tk], HL[:, k, tk], kview("s", WH[:, w, :])[:, k, :],
                                               kview("s", WL[:, w, :])[:, k, :], k == 0, k == KT - 1)
                                return last
                            tile(256, fill)
                    else:
                        toks = lat if (l == 1 and kind == "q") else every
                        for j in range(2):
                            tile(toks.stop - toks.start, standing(w, 0, plain(j * P), toks))
                    c += 1
                for nh in range(1 if l == 0 else 2):
                    for b in range(BLK):
                        if t[0] + b - t0 >= 8:
                            pe.wait_ge(s_qdr, t[0] + b - 7)
                    for kh in range(2):
                        w = split_ready(c)
                        for b in range(BLK):
                            for k in range(4):
                                tk = slice(b * P, (b + 1) * P)
                                last = mm3(PS[:, (t[0] + b) % 8, :], HH[:, kh * 4 + k, tk], HL[:, kh * 4 + k, tk],
                                           kview("m", WH[:, w, :])[:, k, :], kview("m", WL[:, w, :])[:, k, :],
                                           kh == 0 and k == 0, kh == 1 and k == 3)
                            if kh == 1:
                                last.then_inc(s_qps, 1)
                        if kh == 0:
                            last.then_inc(s_khalf, 1)
                        c += 1
                    t[0] += BLK

            def rope(l):
                r0 = 0 if l == 0 else 6
                pe.wait_ge(s_qdr, NT0 if l == 0 else NT0 + NT1)
                for i, (tt, j) in enumerate(rope_tiles(l)):
                    if i >= 2:
                        pe.wait_ge(s_rope, r0 + i - 1)
                    mm(PS[:, i % 2, 0:SEQ], CN[:, C_ROT:C_ROT + P], tt[:, j, CTX:TOK],
                       start=True, stop=True).then_inc(s_rps, 1)

            def attention(l):
                gs = groups[l]
                r_all = 6 if l == 0 else 6 + 16
                pe.wait_ge(s_rope, r_all)

                def scores(gi, b, g):
                    nk = n_keys(l, b)
                    for j in range(4):
                        u = 4 * gi + j
                        if u - 4 * g_base[l] >= 2:
                            pe.wait_ge(s_scd, u - 1)
                        qt, half, kt = head_of(l, g, j)
                        hp = slice(half * HD, half * HD + HD)
                        mm(PS[:, u % 2, 0:nk], QT[hp, qt, b * P:(b + 1) * P], KTT[hp, kt, 0:nk],
                           start=True, stop=True).then_inc(s_sc, 1)

                def weigh(gi, b, g):
                    nk = n_keys(l, b)
                    units = 4 if l == 0 else 2
                    n0 = pts_before(gi)

                    def turn(j):
                        n = n0 + j
                        if l == 0:
                            pe.wait_ge(s_exp, 4 * gi + j + 1)
                        else:
                            pe.wait_ge(s_cmb, 2 * (gi - NG0) + j + 1)
                        if n >= 2:
                            pe.wait_ge(s_ptc, n - 1)
                        for kt in range(nk // P):
                            last = nc.tensor.transpose(PS[:, 2 + n % 2, kt * P:(kt + 1) * P],
                                                       S[:, gi % 2, j if l == 0 else 2 * j, kt * P:(kt + 1) * P],
                                                       ident)
                        last.then_inc(s_ptp, 1)

                    turn(0)
                    for j in range(units):
                        if j + 1 < units:
                            turn(j + 1)
                        if j == 0 and gi >= 2:
                            pe.wait_ge(s_osb, gi - 1)
                        pe.wait_ge(s_ptc, n0 + j + 1)
                        n = HD if l == 0 else P
                        for kt in range(nk // P):
                            last = mm(PS[:, 4 + gi % 2, j * n:(j + 1) * n], PT[:, (n0 + j) % 2, kt * P:(kt + 1) * P],
                                      values(l, g, j)[:, kt, :], start=(kt == 0), stop=(kt == nk // P - 1))
                    last.then_inc(s_ops, 1)

                def turn_block(i):
                    n = i + (0 if l == 0 else 4)
                    if l == 0:
                        pe.wait_ge(s_osb, 4 * (i + 1))
                    else:
                        pe.wait_ge(s_ob, i + 1)
                    if n >= 1:
                        pe.wait_ge(s_otr, n)
                    for half in range(2):
                        for j in range(4):
                            last = nc.tensor.transpose(PS[:, 6 + half, j * P:(j + 1) * P],
                                                       OSB[:, (half * 4 + j) * P:(half * 4 + j + 1) * P], ident)
                    last.then_inc(s_otp, 1)

                scores(g_base[l], *gs[0])
                for i, (b, g) in enumerate(gs):
                    gi = g_base[l] + i
                    if i + 1 < len(gs):
                        scores(gi + 1, *gs[i + 1])
                    weigh(gi, b, g)
                    if g == 3:
                        turn_block(i // 4)

            def project_out(l):
                c = C_OUT0 if l == 0 else C_OUT1
                pe.wait_ge(s_otr, 4 if l == 0 else 6)
                gates(2 * l)
                for nh in range(2):
                    if nh == 1:
                        pe.wait_ge(s_gate, 4 if l == 0 else 10)
                    for kh in range(2):
                        w = split_ready(c)
                        for b in ln_blocks(2 * l):
                            tk = slice(b * P, (b + 1) * P)
                            for k in range(4):
                                last = mm3(PS[:, nh * 4 + b, :], HH[:, kh * 4 + k, tk], HL[:, kh * 4 + k, tk],
                                           kview("m", WH[:, w, :])[:, k, :], kview("m", WL[:, w, :])[:, k, :],
                                           kh == 0 and k == 0, kh == 1 and k == 3)
                            if kh == 1:
                                last.then_inc(s_yps, 1)
                        if kh == 0:
                            last.then_inc(s_khalf, 1)
                        c += 1

            def ffn():
                pe.wait_ge(s_hr, 16)
                gates(1)
                c = C_UP
                for st in range(FT // 2):
                    if st == 1:
                        pe.wait_ge(s_gate, 8)
                    if st >= 2:
                        pe.wait_ge(s_mul, 2 * (st - 1))
                    for gu in range(2):
                        w = split_ready(c)
                        for j in range(2):
                            for k in range(KT):
                                last = mm3(PS[:, st % 2 * 4 + gu * 2 + j, :],
                                           kview("s", WH[:, w, :])[:, k, j * P:(j + 1) * P],
                                           kview("s", WL[:, w, :])[:, k, j * P:(j + 1) * P],
                                           HH[:, k, :], HL[:, k, :], k == 0, k == KT - 1)
                            last.then_inc(s_up, 1)
                        c += 1
                pe.wait_ge(s_mul, FT)
                for j in range(FT // 2):
                    w = split_ready(c)
                    pe.wait_ge(s_gl, j + 1)
                    for k in range(2):
                        for b in range(BLK):
                            tk = slice(b * P, (b + 1) * P)
                            for nh in range(2):
                                last = mm3(PS[:, nh * 4 + b, :], GH[:, j % 2, k, tk], GL[:, j % 2, k, tk],
                                           kview("d", WH[:, w, :])[:, k, nh * 512:(nh + 1) * 512],
                                           kview("d", WL[:, w, :])[:, k, nh * 512:(nh + 1) * 512],
                                           j == 0 and k == 0, j == FT // 2 - 1 and k == 1)
                    last.then_inc(s_dn, 1)
                    c += 1

            def router():
                pe.wait_ge(s_hr, 32)
                pe.wait_ge(s_wr, 16)
                for i in range(2):
                    for k in range(KT):
                        last = mm(PS[:, i, 0:NE], F[:, k, (2 + i) * P:(3 + i) * P], WR[:, k, :],
                                  start=(k == 0), stop=(k == KT - 1))
                    last.then_inc(s_lg, 1)
                gates(3)
                pe.wait_ge(s_gate, 12)
                pe.wait_ge(s_ge, 2)

            def experts():
                NST = EFT // 2
                lat = slice(CTX, TOK)
                with pe.Fori(0, NE) as e:
                    def down(st, q):
                        pe.wait_ge(s_lo, e * CPE + (C_MOE + q + 1))
                        pe.wait_ge(s_mmul, e * NST + (st + 1))
                        if st == 0:
                            pe.wait_ge(s_myd, e * 4 + 4)
                        w = (C_MOE + q) % 2
                        for k in range(2):
                            for i in range(2):
                                tk = slice(k * 256 + i * P, k * 256 + (i + 1) * P)
                                for nh in range(2):
                                    last = mm3(PS[:, 4 + i * 2 + nh, :], AH[:, st % 2, tk], AL[:, st % 2, tk],
                                               kview("d", WH[:, w, :])[:, k, nh * 512:(nh + 1) * 512],
                                               kview("d", WL[:, w, :])[:, k, nh * 512:(nh + 1) * 512],
                                               st == 0 and k == 0, st == NST - 1 and k == 1)
                        last.then_inc(s_mdn, 1)
                    q = 0
                    for st in range(NST):
                        for gu in range(2):
                            pe.wait_ge(s_lo, e * CPE + (C_MOE + q + 1))
                            if gu == 0:
                                pe.wait_ge(s_mrd, e * NST + (st + 1))
                            w = (C_MOE + q) % 2
                            for j in range(2):
                                for k in range(KT):
                                    last = mm3(PS[:, st % 2 * 2 + gu, j * 256:(j + 1) * 256],
                                               kview("s", WH[:, w, :])[:, k, j * P:(j + 1) * P],
                                               kview("s", WL[:, w, :])[:, k, j * P:(j + 1) * P],
                                               HH[:, k, lat], HL[:, k, lat], k == 0, k == KT - 1)
                            last.then_inc(s_mup, 1)
                            q += 1
                        if st >= 1:
                            down(st - 1, q)
                            q += 1
                    down(NST - 1, q)

            h_phase(0)
            project(0)
            rope(0)
            attention(0)
            project_out(0)
            h_phase(1)
            ffn()
            h_phase(2)
            project(1)
            rope(1)
            attention(1)
            project_out(1)
            h_phase(3)
            router()
            experts()

        def expert_used(q, e):
            if q < 2:
                return s_mdn, e * (EFT // 2) + (q + 1)
            what, st = expert_chunk(q - 2)
            if what == "d":
                return s_mdn, e * (EFT // 2) + (st + 3)
            return s_mup, e * EFT + (2 * st + (what == "u") + 1)

        def expert_raw(q):
            slot = q % MRING
            return RAW[:, slot, :] if slot < RING else RAWX[:, slot - RING, :]

        def first_g(st):
            return 0 if st == 0 else 3 * st - 1

        @block.scalar
        def _(act):
            fn = nc.scalar.activation
            done = [0]

            def split(upto):
                for c in range(done[0], min(upto, C_MOE)):
                    act.wait_ge(s_landed[c % RING], 16 * ((N_MOD + c) // RING + 1))
                    if c >= 2:
                        act.wait_ge(*used[c - 2])
                    fn(WH[:, c % 2, :], RAW[:, c % RING, :], ACT.Copy).then_inc(s_hi, 1)
                    done[0] = c + 1

            act.wait_ge(s_vtc, 1)
            for s in range(2):
                fn(ST[:, :, s], VT[:, 96 + 8 * s:104 + 8 * s], ACT.Silu).then_inc(s_silu, 1)
            for n in range(DEPTH * NB_MOD):
                act.wait_ge(s_modused, 2 * n + 2)
                fn(ROW[:, n % 2, :], PS[0:2, n % 2, :], ACT.Copy).then_inc(s_modrow, 1)
            act.wait_ge(s_lam, 1)
            fn(LT[:, 2:4], LT[:, 0:2], ACT.Exp).then_inc(s_lame, 1)

            def h_phase(h):
                l, seg = h // 2, 3 * (h % 2)
                if h == 0:
                    act.wait_ge(s_modc, 2)
                for dt in range(KT):
                    act.wait_ge(s_hps, 8 * h + dt + 1)
                    for s, lo in ((1, 0), (0, CTX)):
                        if h == 3 and s == 1:
                            continue
                        last = fn(F[:, dt, lo:lo + 256], PS[:, dt % 4, lo:lo + 256], ACT.Identity,
                                  bias=MODC[:, l, seg * 8 + dt, s:s + 1],
                                  scale=MODC[:, l, (seg + 1) * 8 + dt, s:s + 1])
                    last.then_inc(s_hf, 1)

            def project(l):
                t = 0 if l == 0 else NT0
                for c, tiles in projection(l):
                    split(c + 2)
                    for cols, dst in tiles:
                        act.wait_ge(s_qps, t + 1)
                        if isinstance(dst, str):
                            for kv in range(A_KV):
                                for half in range(2):
                                    last = fn(KTT[half * HD:(half + 1) * HD, kv, :],
                                              PS[kv * HD:(kv + 1) * HD, t % 8, cols], ACT.Copy)
                            last.then_inc(s_qdr, 1)
                        else:
                            fn(dst, PS[:, t % 8, cols], ACT.Copy).then_inc(s_qdr, 1)
                        t += 1

            def attention(l):
                gs = groups[l]

                def exps(gi, b, j):
                    nk = n_keys(l, b)
                    if j == 0:
                        act.wait_ge(s_nm, gi + 1)
                    fn(S[:, gi % 2, j, 0:nk], S[:, gi % 2, j, 0:nk], ACT.Exp, bias=NM(gi)[:, j:j + 1],
                       accum_out=SU(gi)[:, j:j + 1]).then_inc(s_exp, 1)

                def sinks(gi, g):
                    if l == 0 and g < 2:
                        fn(SE(gi), SD(gi), ACT.Exp).then_inc(s_sink, 1)

                for j in range(4):
                    exps(g_base[l], gs[0][0], j)
                sinks(g_base[l], gs[0][1])
                for i, (b, g) in enumerate(gs):
                    gi = g_base[l] + i
                    units = 4 if l == 0 else 2
                    for j in range(4):
                        if j < units:
                            n = pts_before(gi) + j
                            act.wait_ge(s_ptp, n + 1)
                            nk = n_keys(l, b)
                            fn(PT[:, n % 2, 0:nk], PS[:, 2 + n % 2, 0:nk], ACT.Copy).then_inc(s_ptc, 1)
                        if i + 1 < len(gs):
                            exps(gi + 1, gs[i + 1][0], j)
                    if i + 1 < len(gs):
                        sinks(gi + 1, gs[i + 1][1])
                    if g == 3:
                        if l == 1:
                            act.wait_ge(s_ssq, i // 4 + 1)
                            fn(SS2, SS, ACT.Sqrt).then_inc(s_ssr, 1)
                        n = i // 4 + (0 if l == 0 else 4)
                        act.wait_ge(s_otp, n + 1)
                        for half in range(2):
                            fn(HH[:, half * 4:half * 4 + 4, b * P:(b + 1) * P],
                               PS[:, 6 + half, :].rearrange("p (j q) -> p j q", j=4), ACT.Copy).then_inc(s_oth, 1)

            def gates(p):
                n = (0, 4, 8, 10)[p]
                for s in ((0, 1) if p < 2 else (1,)):
                    for half in range(2):
                        act.wait_ge(s_gps, n + 1)
                        fn(GATE[:, s, half * 512:(half + 1) * 512], PS[:, 4 + s * 2 + half, :], ACT.Copy)\
                            .then_inc(s_gate, 1)
                        n += 1

            def norm(p):
                act.wait_ge(s_var, p + 1)
                n = len(ln_blocks(p))
                fn(SQ[:, 0:n], SV[:, 0:n], ACT.Sqrt).then_inc(s_std, 1)

            def mixer(l):
                h_phase(2 * l)
                project(l)
                attention(l)
                gates(2 * l)
                c0 = C_OUT0 if l == 0 else C_OUT1
                split(c0 + 6)
                norm(2 * l)

            split(2)
            mixer(0)
            h_phase(1)
            gates(1)
            for st in range(FT // 2):
                cg = C_UP + 2 * st
                split(cg + 2)
                for j in range(2):
                    act.wait_ge(s_up, 4 * st + j + 1)
                    if st >= 1:
                        act.wait_ge(s_mul, 2 * st - 1 + j)
                    fn(T[:, j, :], PS[:, st % 2 * 4 + j, :], ACT.Silu).then_inc(s_silg, 1)
                    if j == 0:
                        split(cg + 3)
                if st < FT // 2 - 1:
                    split(cg + 4)
            split(C_DN + 2)

            def product_hi(j):
                if j >= 2:
                    act.wait_ge(s_dn, j - 1)
                act.wait_ge(s_mul, 2 * j + 2)
                fn(GH[:, j % 2, :, :], GT[:, 2 * j:2 * j + 2, :], ACT.Copy).then_inc(s_gh, 1)

            product_hi(0)
            product_hi(1)
            for j in range(FT // 2):
                split(C_DN + j + 3)
                if j + 2 < FT // 2:
                    product_hi(j + 2)
            norm(1)
            mixer(1)
            h_phase(3)
            for i in range(2):
                act.wait_ge(s_gx, i + 1)
                fn(EV[:, 1:2], EV[:, 0:1], ACT.Exp).then_inc(s_ge, 1)
            gates(3)
            act.wait_ge(*used[C_MOE - 1])
            act.wait_ge(s_myd, 4)
            with act.Fori(0, NE) as e:
                for q in range(CPE):
                    act.wait_ge(s_mland[q % MRING], e * (16 * CPE // MRING) + 16 * (q // MRING + 1))
                    act.wait_ge(*expert_used(q, e))
                    fn(WH[:, q % 2, :], expert_raw(q), ACT.Copy).then_inc(s_hi, 1)
                    for st in range(EFT // 2):
                        if q == first_g(st) + 2:
                            act.wait_ge(s_mup, e * EFT + (2 * st + 1))
                            act.wait_ge(s_mrd, e * (EFT // 2) + (st + 1))
                            fn(MT[:, st % 2, :], PS[:, st % 2 * 2, :], ACT.Silu).then_inc(s_msil, 1)
            norm(3)

        @block.vector
        def _(dve):
            v = nc.vector
            done = [0]
            chain = [0]
            term = [0]

            def link(ins):
                ins.then_inc(s_dve, 1)
                chain[0] += 1
                dve.wait_ge(s_dve, term[0] + chain[0])

            def split(upto):
                for c in range(done[0], min(upto, C_MOE)):
                    dve.wait_ge(s_hi, c + 1)
                    v.tensor_tensor(WL[:, c % 2, :], RAW[:, c % RING, :], WH[:, c % 2, :].bitcast(F32),
                                    ALU.subtract).then_inc(s_lo, 1)
                    done[0] = c + 1

            dve.wait_ge(s_vt, 1)
            v.tensor_copy(VT[:, :], PS[:, 7, 0:112]).then_inc(s_vtc, 1)
            dve.wait_ge(s_vtc, 1)
            dve.wait_ge(s_small, 48)
            lp = LAMP[:, :].rearrange("p (a b c) -> p a b c", a=2, b=2)
            prod = SM[:, 240:368].rearrange("p (a c) -> p a c", a=2)
            link(v.tensor_tensor(prod, lp[:, :, 0, :], lp[:, :, 1, :], ALU.mult))
            v.reduce_sum(LT[:, 0:2], prod, AX.X).then_inc(s_lam, 1)
            link(v.tensor_scalar(SUBL[:, :], SUBL[:, :], 1.0 - LAM_INIT, None, ALU.mult))
            dve.wait_ge(s_bl, 16 * ROWS * ROWS)
            for b in range(2):
                rows = BIAS[:, b, :, :].rearrange("p h (r c) -> p (h r) c", r=ROWS)
                mask = CN[:, C_MB:C_MB + GRID_W].unsqueeze(1).to_broadcast([P, B_HEADS * ROWS, GRID_W])
                link(v.scalar_tensor_tensor(rows, rows, 1.0 / SCALE, mask, ALU.mult, ALU.add))
            for l in range(DEPTH):
                dve.wait_ge(s_modcol, l + 1)
                ps = PS[:, 2 + l, 0:96].rearrange("p (n s) -> p n s", s=2)
                link(v.tensor_tensor(MODC[:, l, :, :], ps, VT[:, l * 48:(l + 1) * 48].unsqueeze(2)
                                     .to_broadcast([P, 48, 2]), ALU.add))
                link(v.tensor_scalar(MODC[:, l, 8:16, :], MODC[:, l, 8:16, :], 1.0, None, ALU.add))
                v.tensor_scalar(MODC[:, l, 32:40, :], MODC[:, l, 32:40, :], 1.0, None, ALU.add).then_inc(s_modc, 1)
            dve.wait_ge(s_lame, 1)
            link(v.tensor_tensor(LAM, LT[:, 3:4], LT[:, 2:3], ALU.subtract))
            link(v.tensor_scalar(LAM, LAM, -LAM_INIT, None, ALU.add))

            def h_phase(h):
                toks = slice(CTX, TOK) if h == 3 else slice(0, TOK)
                for dt in range(KT):
                    dve.wait_ge(s_hf, 8 * h + dt + 1)
                    link(v.tensor_copy(HH[:, dt, toks], F[:, dt, toks]))
                    v.tensor_tensor(HL[:, dt, toks], F[:, dt, toks], HH[:, dt, toks].bitcast(F32),
                                    ALU.subtract).then_inc(s_hr, 1)

            def rope(l):
                n = 0 if l == 0 else 6
                cos, sin = CN[:, C_COS:C_COS + SEQ], CN[:, C_SIN:C_SIN + SEQ]
                for i, (tt, j) in enumerate(rope_tiles(l)):
                    t = tt[:, j, CTX:TOK]
                    dve.wait_ge(s_rps, n + i + 1)
                    if i >= 1:
                        dve.wait_ge(s_rope, n + i)
                    link(v.tensor_tensor(OSB[:, 0:SEQ], PS[:, i % 2, 0:SEQ], sin, ALU.mult))
                    link(v.tensor_tensor(t, t, cos, ALU.mult))
                    v.tensor_tensor(t, t, OSB[:, 0:SEQ], ALU.add).then_inc(s_rope, 1)
                dve.wait_ge(s_rope, n + len(rope_tiles(l)))

            def attention(l):
                gs = groups[l]
                n_sink = [0]
                if l == 0:
                    dve.wait_ge(s_zero, 1)

                def front(gi, b, g):
                    nk = n_keys(l, b)
                    two = l == 0 and b >= 2
                    for j in range(4):
                        u = 4 * gi + j
                        dve.wait_ge(s_sc, u + 1)
                        if j == 0 and gi - 2 >= g_base[l]:
                            dve.wait_ge(s_ptp, pts_before(gi - 1))
                        mx = MX(gi)
                        if two:
                            add = CN[:, C_MA + (b - 2) * SEQ:C_MA + (b - 1) * SEQ] if g < 2 else \
                                BIAS[:, b - 2, 4 * (g - 2) + j, :]
                            v.tensor_tensor_reduce(out=S[:, gi % 2, j, CTX:TOK], in0=PS[:, u % 2, CTX:TOK], in1=add,
                                                   scale=SCALE, scalar=-3e38, op0=ALU.add, op1=ALU.max,
                                                   accum_out=mx[:, 2 * j:2 * j + 1])
                            v.tensor_tensor_reduce(out=S[:, gi % 2, j, 0:CTX], in0=PS[:, u % 2, 0:CTX],
                                                   in1=ZERO[:, 0:CTX], scale=SCALE, scalar=-3e38, op0=ALU.add,
                                                   op1=ALU.max, accum_out=mx[:, 2 * j + 1:2 * j + 2])\
                                .then_inc(s_scd, 1)
                        else:
                            v.tensor_tensor_reduce(out=S[:, gi % 2, j, 0:nk], in0=PS[:, u % 2, 0:nk],
                                                   in1=ZERO[:, 0:nk], scale=SCALE, scalar=-3e38, op0=ALU.add,
                                                   op1=ALU.max, accum_out=mx[:, j:j + 1]).then_inc(s_scd, 1)
                    dve.wait_ge(s_scd, 4 * gi + 4)
                    top = MX(gi)[:, 0:4]
                    if two:
                        link(v.reduce_max(MM(gi), MX(gi).rearrange("p (j t) -> p j t", t=2), AX.X))
                        top = MM(gi)
                    if l == 0 and g < 2:
                        link(v.tensor_tensor(MM(gi), top, SINK[:, 4 * g:4 * g + 4], ALU.max))
                        top = MM(gi)
                        link(v.tensor_tensor(SD(gi), SINK[:, 4 * g:4 * g + 4], top, ALU.subtract))
                    v.tensor_scalar(NM(gi), top, -1.0, None, ALU.mult).then_inc(s_nm, 1)

                def back(i, gi, b, g):
                    dve.wait_ge(s_exp, 4 * gi + 4)
                    if l == 0:
                        if g < 2:
                            n_sink[0] += 1
                            dve.wait_ge(s_sink, n_sink[0])
                            link(v.tensor_tensor(SU(gi), SU(gi), SE(gi), ALU.add))
                        link(v.reciprocal(RI(gi), SU(gi)))
                        dve.wait_ge(s_ops, gi + 1)
                        if g == 0 and gi >= 4:
                            dve.wait_ge(s_otp, gi // 4)
                        v.tensor_tensor(OSB[:, g * 256:(g + 1) * 256].rearrange("p (j d) -> p j d", j=4),
                                        PS[:, 4 + gi % 2, 0:256].rearrange("p (j d) -> p j d", j=4),
                                        RI(gi).unsqueeze(2).to_broadcast([P, 4, HD]), ALU.mult)\
                            .then_inc(s_osb, 1)
                    else:
                        dve.wait_ge(s_ops, gi + 1)
                        if g == 0:
                            dve.wait_ge(s_otp, 4 + i // 4)
                        v.tensor_copy(OSB[:, g * 256:(g + 1) * 256], PS[:, 4 + gi % 2, 0:256]).then_inc(s_osb, 1)

                def combine(gi):
                    dve.wait_ge(s_exp, 4 * gi + 4)
                    link(v.reciprocal(RI(gi), SU(gi)))
                    r = RI(gi).rearrange("p (h i) -> p h i", i=2)
                    link(v.tensor_scalar(r[:, :, 1], r[:, :, 1], LAM, None, ALU.mult))
                    for h in range(2):
                        p0, p1 = S[:, gi % 2, 2 * h, :], S[:, gi % 2, 2 * h + 1, :]
                        link(v.tensor_scalar(p1, p1, RI(gi)[:, 2 * h + 1:2 * h + 2], None, ALU.mult))
                        v.scalar_tensor_tensor(p0, p0, RI(gi)[:, 2 * h:2 * h + 1], p1, ALU.mult, ALU.add)\
                            .then_inc(s_cmb, 1)

                front(g_base[l], *gs[0])
                for i, (b, g) in enumerate(gs):
                    gi = g_base[l] + i
                    if l == 1:
                        combine(gi)
                    if i + 1 < len(gs):
                        front(gi + 1, *gs[i + 1])
                    back(i, gi, b, g)
                    if g == 3:
                        dve.wait_ge(s_osb, gi + 1)
                        n = i // 4 + (0 if l == 0 else 4)
                        if l == 1:
                            ov = OSB[:, :].rearrange("p (h e) -> p h e", h=C_HEADS)
                            link(v.tensor_tensor(TQ[:, :], OSB[:, :], OSB[:, :], ALU.mult))
                            link(v.reduce_sum(SS, TQ[:, :].rearrange("p (h e) -> p h e", h=C_HEADS), AX.X))
                            v.tensor_scalar(SS, SS, 1.0 / P, EPS, ALU.mult, ALU.add).then_inc(s_ssq, 1)
                            dve.wait_ge(s_ssr, i // 4 + 1)
                            link(v.reciprocal(SS, SS2))
                            link(v.tensor_tensor(ov, ov, SS.unsqueeze(2).to_broadcast([P, C_HEADS, P]), ALU.mult))
                            v.tensor_tensor(ov, ov, SUBL[:, :].unsqueeze(1).to_broadcast([P, C_HEADS, P]),
                                            ALU.mult).then_inc(s_ob, 1)
                        dve.wait_ge(s_oth, 2 * n + 2)
                        for half in range(2):
                            dst = slice(half * 4, half * 4 + 4)
                            last = v.tensor_tensor(HL[:, dst, b * P:(b + 1) * P],
                                                   PS[:, 6 + half, :].rearrange("p (j q) -> p j q", j=4),
                                                   HH[:, dst, b * P:(b + 1) * P].bitcast(F32), ALU.subtract)
                        last.then_inc(s_otr, 1)

            def norm(p):
                bs = ln_blocks(p)
                dve.wait_ge(s_gate, (4, 8, 10, 12)[p])
                for nh in range(2):
                    for i, b in enumerate(bs):
                        half = slice(nh * 512, (nh + 1) * 512)
                        if p == 1:
                            dve.wait_ge(s_dn, FT // 2)
                        elif p < 3:
                            dve.wait_ge(s_yps, y_before[p] + nh * len(bs) + i + 1)
                        y = ACC[:, i * 2 + nh, :] if p == 3 else PS[:, nh * 4 + b, :]
                        link(v.tensor_tensor(TMP[:, :], y, GATE[:, b // 2, half], ALU.mult))
                        link(v.scalar_tensor_tensor(X[:, b, half], X[:, b, half], ALPHA, TMP[:, :],
                                                    ALU.mult, ALU.add))
                for i, b in enumerate(bs):
                    for nh in range(2):
                        link(v.bn_stats(ST6[:, i, nh * 6:nh * 6 + 6], X[:, b, nh * 512:(nh + 1) * 512]))
                    link(v.bn_aggr(MV[:, i, :], ST6[:, i, :]))
                n = len(bs)
                v.tensor_scalar(SV[:, 0:n], MV[:, 0:n, 1], EPS, None, ALU.add).then_inc(s_var, 1)
                dve.wait_ge(s_std, p + 1)
                link(v.reciprocal(RS[:, 0:n], SQ[:, 0:n]))
                dve.wait_ge(s_lnr, 32 * (p + 1))
                for i, b in enumerate(bs):
                    xb = X[:, b, :]
                    link(v.tensor_scalar(xb, xb, MV[:, i, 0:1], RS[:, i:i + 1], ALU.subtract, ALU.mult))
                    link(v.tensor_tensor(xb, xb, LNR[:, 0, :], ALU.mult))
                    v.tensor_tensor(xb, xb, LNR[:, 1, :], ALU.add).then_inc(s_ln, 1)

            def mixer(l):
                h_phase(2 * l)
                for c, _ in projection(l):
                    split(c + 2)
                rope(l)
                attention(l)
                split((C_OUT0 if l == 0 else C_OUT1) + 6)
                norm(2 * l)

            split(2)
            mixer(0)
            h_phase(1)
            for st in range(FT // 2):
                cg = C_UP + 2 * st
                split(cg + 3)
                for j in range(2):
                    if j == 1 and st < FT // 2 - 1:
                        split(cg + 4)
                    dve.wait_ge(s_silg, 2 * st + j + 1)
                    dve.wait_ge(s_up, 4 * st + 3 + j)
                    v.tensor_tensor(GT[:, 2 * st + j, :], T[:, j, :], PS[:, st % 2 * 4 + 2 + j, :],
                                    ALU.mult).then_inc(s_mul, 1)
            split(C_DN + 2)

            def product_lo(j):
                dve.wait_ge(s_gh, j + 1)
                v.tensor_tensor(GL[:, j % 2, :, :], GT[:, 2 * j:2 * j + 2, :], GH[:, j % 2, :, :].bitcast(F32),
                                ALU.subtract).then_inc(s_gl, 1)

            product_lo(0)
            product_lo(1)
            for j in range(FT // 2):
                split(C_DN + j + 3)
                if j + 2 < FT // 2:
                    product_lo(j + 2)
            norm(1)
            mixer(1)
            h_phase(3)
            for i in range(2):
                dve.wait_ge(s_lg, i + 1)
                link(v.tensor_copy(LG, PS[:, i, 0:NE]))
                link(v.max(M8, LG))
                link(v.max_index(IDX[:, :], M8, LG))
                link(v.tensor_copy(IF, IDX[:, :]))
                v.tensor_tensor(EV[:, 0:1], M8[:, 1:2], M8[:, 0:1], ALU.subtract).then_inc(s_gx, 1)
                dve.wait_ge(s_ge, i + 1)
                link(v.tensor_scalar(EV[:, 2:3], EV[:, 1:2], 1.0, None, ALU.add))
                link(v.reciprocal(EV[:, 3:4], EV[:, 2:3]))
                link(v.tensor_tensor(EV[:, 4:5], EV[:, 1:2], EV[:, 3:4], ALU.mult))
                iota = CN[:, C_IOTA:C_IOTA + NE]
                link(v.tensor_scalar(OH, iota, IF[:, 0:1], EV[:, 3:4], ALU.is_equal, ALU.mult))
                link(v.tensor_scalar(GW[:, i, :], iota, IF[:, 1:2], EV[:, 4:5], ALU.is_equal, ALU.mult))
                link(v.tensor_tensor(GW[:, i, :], GW[:, i, :], OH, ALU.add))
            v.memset(ACC[:, 0, :], 0.0).then_inc(s_mrd, 2)
            v.memset(ACC[:, 1, :], 0.0).then_inc(s_mdn, 2)
            v.memset(ACC[:, 2:4, :], 0.0).then_inc(s_myd, 4)
            dve.wait_ge(s_myd, 4)
            NST = EFT // 2
            links = NST
            with dve.Fori(0, NE) as e:
                start = chain[0]
                term[0] = e * links
                for q in range(CPE):
                    dve.wait_ge(s_hi, e * CPE + (C_MOE + q + 1))
                    v.tensor_tensor(WL[:, q % 2, :], expert_raw(q), WH[:, q % 2, :].bitcast(F32),
                                    ALU.subtract).then_inc(s_lo, 1)
                    for st in range(NST):
                        if q == first_g(st) + 3:
                            dve.wait_ge(s_msil, e * NST + (st + 1))
                            dve.wait_ge(s_mup, e * EFT + (2 * st + 2))
                            v.tensor_tensor(AF[:, st % 2, :], MT[:, st % 2, :], PS[:, st % 2 * 2 + 1, :],
                                            ALU.mult).then_inc(s_mrd, 1)
                            dve.wait_ge(s_mrd, e * NST + (st + 3))
                            dve.wait_ge(s_mdn, e * NST + (st + 1))
                            link(v.tensor_copy(AH[:, st % 2, :], AF[:, st % 2, :]))
                            v.tensor_tensor(AL[:, st % 2, :], AF[:, st % 2, :], AH[:, st % 2, :].bitcast(F32),
                                            ALU.subtract).then_inc(s_mmul, 1)
                dve.wait_ge(s_mdn, e * NST + (NST + 2))
                for i in range(2):
                    for nh in range(2):
                        a = ACC[:, i * 2 + nh, :]
                        v.scalar_tensor_tensor(a, PS[:, 4 + i * 2 + nh, :], GW[:, i, bass.ds(e, 1)], a,
                                               ALU.mult, ALU.add).then_inc(s_myd, 1)
                assert chain[0] - start == links
            chain[0] = start + NE * links
            term[0] = 0
            dve.wait_ge(s_myd, 4 * NE + 4)
            norm(3)


INPUTS = ["x", "ctx", "vecs", "consts", "w_mod", "ln_g", "ln_b", "w_in_ab", "w_out_ab", "sink_a", "rpb_b",
          "w_in_c", "w_out_c", "lam_c", "subln_c", "w_ffn_up", "w_ffn_down", "w_router", "w_exp_up", "w_exp_down"]


def kernel(**inputs):
    import concourse.bacc as bacc
    from concourse.bass_utils import run_bass_kernel_spmd

    given = {k: np.ascontiguousarray(v) for k, v in inputs.items()}
    given["vecs"] = np.concatenate([given["b_mod"].reshape(-1, P), given["c"].reshape(-1, P),
                                    given["c_ctx"].reshape(-1, P)], axis=0)
    given["consts"] = shape_constants()
    nc = bacc.Bacc("TRN2", target_bir_lowering=False, num_devices=1)
    arrays, args = {}, []
    for name in INPUTS:
        a = given[name]
        arrays["in_" + name] = a
        args.append(nc.dram_tensor("in_" + name, a.shape, mybir.dt.from_np(a.dtype), kind="ExternalInput").ap())
    args.append(nc.dram_tensor("out_0", (1, SEQ, D), F32, kind="ExternalOutput").ap())
    trunk(nc, *args)
    return run_bass_kernel_spmd(nc, [arrays], core_ids=[0]).results[0]["out_0"]
```

```python
import math
from contextlib import ExitStack

import numpy as np

import concourse.bass as bass
from concourse import mybir

F32 = mybir.dt.float32
F32R = mybir.dt.float32r
U32 = mybir.dt.uint32
I32 = mybir.dt.int32
ALU = mybir.AluOpType
ACT = mybir.ActivationFunctionType
AX = mybir.AxisListType

P = 128
D = 1024
KT = D // P
SEQ = 256
CTX = 256
BLK = 4
TOK = BLK * P
DEPTH = 2
HD = 64
GRID_W = 64
ROWS = SEQ // GRID_W
A_HEADS = 8
A_KV = 2
B_HEADS = 8
C_HEADS = 8
KH_MAX = 8
NKW = 16
WINDOW = 128
FF = 2816
FT = FF // P
NE = 8
EFF = 3584
EFT = EFF // P
EPS = 1e-5
ALPHA = (2 * DEPTH) ** 0.25
SCALE = HD ** -0.5
MASK = -1e30 / SCALE
LAM_INIT = 0.8 - 0.6 * math.exp(-0.3)

CW = 2048
NB_MOD = 6 * D // 512
N_MOD = NB_MOD * 2
MOD_ATT, MOD_GAP = 8, 2
RING = 4
MRING = 7
MSPLIT = 3
DR = 2 * ROWS - 1
DC = 2 * NKW - 1
ZL = 2 * GRID_W - 1

C_ID, C_ROT, C_MA, C_MB, C_COS, C_SIN, C_IOTA, C_ADD = 0, 128, 256, 768, 832, 1088, 1344, 1352
C_ALL = 1354
M_TRI, M_IOTA, M_ONE, M_THR, M_C, M_E = 0, 128, 256, 384, 385, 386
CM_ALL = 387


def shape_constants():
    cn = np.zeros((P, C_ALL), np.float32)
    cn[:, C_ID:C_ID + P] = np.eye(P, dtype=np.float32)
    rot = np.zeros((P, P), np.float32)
    for m in range(P):
        q = (m % 64) // 16
        if q % 2 == 0:
            rot[m, m + 16] = -1.0
        else:
            rot[m, m - 16] = 1.0
    cn[:, C_ROT:C_ROT + P] = rot.T
    for b in range(2):
        qi = b * P + np.arange(P)[:, None]
        ki = np.arange(SEQ)[None, :]
        cn[:, C_MA + b * SEQ:C_MA + (b + 1) * SEQ] = np.where(np.abs(qi - ki) <= WINDOW, 0.0, MASK)
    col = (np.arange(P) % GRID_W)[:, None]
    start = np.clip(col - NKW // 2, 0, GRID_W - NKW)
    kc = np.arange(GRID_W)[None, :]
    cn[:, C_MB:C_MB + GRID_W] = np.where((kc >= start) & (kc < start + NKW), 0.0, MASK)
    t = np.arange(SEQ)
    half = HD // 2
    inv = np.float32(10000.0) ** (-np.arange(0, half, 2, dtype=np.float32) / np.float32(half))
    ar = (t // GRID_W).astype(np.float32)[:, None] * inv
    ac = (t % GRID_W).astype(np.float32)[:, None] * inv
    ang = np.concatenate([ar, ar, ac, ac], -1).astype(np.float32)
    ang = np.concatenate([ang, ang], -1).T
    cn[:, C_COS:C_COS + SEQ] = np.cos(ang)
    cn[:, C_SIN:C_SIN + SEQ] = np.sin(ang)
    cn[0:4, C_ADD:C_ADD + 2] = np.tile(np.eye(2, dtype=np.float32), (2, 1))
    cn[:, C_IOTA:C_IOTA + 8] = np.arange(8, dtype=np.float32)
    return cn


def item_constants():
    cm = np.zeros((P, CM_ALL), np.float32)
    cm[:, M_TRI:M_TRI + P] = np.triu(np.ones((P, P), np.float32), 1)
    cm[:, M_IOTA:M_IOTA + P] = np.arange(P, dtype=np.float32)
    cm[:, M_ONE:M_ONE + P] = 1.0
    c = np.arange(2 * NE)
    cm[0:2 * NE, M_THR] = P * (c % 2)
    cm[0:2 * NE, M_C] = c
    cm[0:2 * NE, M_E] = c // 2
    return cm


def trunk(nc, x, ctx_in, vecs, consts, item_consts, w_mod, ln_g, ln_b, w_in_ab, w_out_ab, sink_a, rpb, w_in_c,
          w_out_c, lam_c, subln, w_up, w_down, w_router, w_eup, w_edown, out):
    ctx = ExitStack()
    with ctx:
        base = 16512

        def sb(name, shape, dt, off):
            return nc.alloc_sbuf_tensor_at(name, shape, dt, offset=base + off)

        def sem(name):
            return ctx.enter_context(nc.semaphore(name))

        K = 1024
        X = sb("X", [P, BLK, D], F32, 0)
        HH = sb("HH", [P, KT, TOK], F32R, 16 * K)
        HL = sb("HL", [P, KT, TOK], F32R, 32 * K)
        ROWS_AT = sb("ROWS_AT", [P, KT, TOK], F32, 32 * K)
        RAW = sb("RAW", [P, RING, CW], F32, 48 * K)
        WH = sb("WH", [P, 2, CW], F32R, 80 * K)
        WL = sb("WL", [P, 2, CW], F32R, 96 * K)
        CN = sb("CN", [P, C_ALL], F32, 112 * K)
        o = 112 * K + 5440
        assert 4 * C_ALL <= 5440
        ZERO = sb("ZERO", [P, 512], F32, o); o += 2048
        VT = sb("VT", [P, 112], F32, o); o += 448
        ST = sb("ST", [P, KT, 2], F32, o); o += 64
        STS = sb("STS", [P, KT, 4], F32R, o); o += 128
        MODC = sb("MODC", [P, DEPTH, 48, 2], F32, o); o += 768
        SINK = sb("SINK", [P, A_HEADS], F32, o); o += 32
        LAMP = sb("LAMP", [P, 4 * HD], F32, o); o += 1024
        SUBL = sb("SUBL", [P, P], F32, o); o += 512
        SM = sb("SM", [P, 512], F32, o); o += 2048
        IDX = sb("IDX", [P, 8], U32, o); o += 32
        R0 = 125 * K
        assert o <= R0, o
        F = sb("F", [P, KT, TOK], F32, R0)
        QT = sb("QT", [P, 8, TOK], F32, R0)
        KTT = sb("KTT", [P, 8, TOK], F32, R0 + 16 * K)
        V0 = sb("V0", [P, BLK, 640], F32, R0 + 32 * K)
        BIAS = sb("BIAS", [P, 2, B_HEADS, SEQ], F32, R0 + 42 * K)
        V1 = sb("V1", [P, BLK, D], F32, R0 + 32 * K)
        TQ = sb("TQ", [P, D], F32, R0 + 48 * K)
        S = sb("S", [P, 2, 4, 512], F32, R0 + 58 * K)
        PT = sb("PT", [P, 2, 512], F32, R0 + 74 * K)
        OSB = sb("OSB", [P, D], F32, R0 + 78 * K)
        VR = sb("VR", [112, P], F32, R0 + 62 * K)
        ZP = sb("ZP", [B_HEADS * DR, ZL + 1], F32, R0 + 64 * K)
        GT = sb("GT", [P, FT, TOK], F32, R0)
        GH = sb("GH", [P, 2, 2, TOK], F32R, R0 + 44 * K)
        GL = sb("GL", [P, 2, 2, TOK], F32R, R0 + 52 * K)
        T = sb("T", [P, 2, 512], F32, R0 + 60 * K)
        GATE = sb("GATE", [P, 2, D], F32, R0 + 64 * K)
        LNR = sb("LNR", [P, 2, D], F32, R0 + 72 * K)
        TMP = sb("TMP", [P, 512], F32, R0 + 80 * K)
        WR = sb("WR", [P, KT, NE], F32, R0 + 81 * K + 1024)
        HE = sb("HE", [P, KT, P], F32R, 16 * K)
        LE = sb("LE", [P, KT, P], F32R, 20 * K)
        RAWX = sb("RAWX", [P, MRING - RING, CW], F32, 24 * K)
        ACC = sb("ACC", [P, 4, 512], F32, R0)
        WHX = sb("WHX", [P, CW], F32R, R0 + 16 * K)
        WLX = sb("WLX", [P, CW], F32R, R0 + 24 * K)
        AF = sb("AF", [P, 2, 512], F32, R0 + 32 * K)
        TH = sb("TH", [P, 2, 512], F32R, R0 + 36 * K)
        TL = sb("TL", [P, 2, 512], F32R, R0 + 40 * K)
        FE = sb("FE", [P, KT, P], F32, R0 + 44 * K)
        SEL = sb("SEL", [P, 2, P], F32, R0 + 48 * K)
        SELG = sb("SELG", [P, 2, P], F32, R0 + 49 * K)
        BACK = sb("BACK", [P, 2 * P], F32, R0 + 50 * K)
        Y = sb("Y", [P, 2, 512], F32, R0 + 52 * K)
        MT = sb("MT", [P, 2, 512], F32, R0 + 56 * K)
        CM = sb("CM", [P, CM_ALL], F32, R0 + 60 * K)
        SR = sb("SR", [P, 256], F32, R0 + 60 * K + 2048)
        TAB = sb("TAB", [1, 48], I32, R0 + 60 * K + 3072)

        MX = lambda g: SM[:, (g % 2) * 8:(g % 2) * 8 + 8]
        MM = lambda g: SM[:, 16 + (g % 2) * 4:20 + (g % 2) * 4]
        NM = lambda g: SM[:, 24 + (g % 2) * 4:28 + (g % 2) * 4]
        SU = lambda g: SM[:, 32 + (g % 2) * 4:36 + (g % 2) * 4]
        SD = lambda g: SM[:, 40 + (g % 2) * 4:44 + (g % 2) * 4]
        SE = lambda g: SM[:, 48 + (g % 2) * 4:52 + (g % 2) * 4]
        RI = lambda g: SM[:, 56 + (g % 2) * 4:60 + (g % 2) * 4]
        LT = SM[:, 64:72]
        LAM = SM[:, 72:73]
        SS = SM[:, 80:88]
        SS2 = SM[:, 88:96]
        ST6 = SM[:, 96:144].rearrange("p (b s) -> p b s", b=4)
        MV = SM[:, 144:152].rearrange("p (b s) -> p b s", b=4)
        SV = SM[:, 152:156]
        SQ = SM[:, 156:160]
        RS = SM[:, 160:164]
        NMR = SM[:, 164:168]
        LG = SM[:, 176:184]
        M8 = SM[:, 184:192]
        EV = SM[:, 192:200]
        IF = SM[:, 200:208]
        OH = SM[:, 208:216]
        MASKS = SR[:, 0:16].rearrange("p (b e) -> p b e", b=2)
        MASK2 = SR[:, 16:48].rearrange("p (b c) -> p b c", b=2)
        POS = SR[:, 48:80].rearrange("p (b c) -> p b c", b=2)
        GC = SR[:, 80:112].rearrange("p (b c) -> p b c", b=2)
        PRES = SR[0:16, 112:113]
        ISEL = SR[0:16, 128:144]
        GW = SM[:, 224:240].rearrange("p (b e) -> p b e", b=2)

        PS = ctx.enter_context(nc.psum_tensor("PS", [P, 8, 512], F32))
        fbias = nc.dram_tensor("bias_rows", [B_HEADS * DR, GRID_W, ZL], F32, kind="Internal").ap()

        ident = CN[:, C_ID:C_ID + P]

        def mod_row(n, parts=2):
            return ROWS_AT[0:parts, n % 2 * 4:n % 2 * 4 + 4, TOK - P:TOK]

        chunks = []

        def stat_chunk(w, n0):
            chunks.append(("s", w[:, n0:n0 + 256].rearrange("(k p) n -> p k n", p=P)))

        def move_chunk(w, n0, kh):
            chunks.append(("m", w[kh * 512:(kh + 1) * 512, n0:n0 + 512].rearrange("(k p) n -> p k n", p=P)))

        wi = w_in_ab[0]
        for n0 in (0, 256, 512, 768, 1024, 1280, 1536):
            stat_chunk(wi, n0)
        move_chunk(wi, 1792, 0)
        move_chunk(wi, 1792, 1)
        C_OUT0 = len(chunks)
        for nh in range(2):
            for kh in range(2):
                move_chunk(w_out_ab[0], nh * 512, kh)
        C_UP = len(chunks)
        for st in range(FT // 2):
            stat_chunk(w_up[0], st * 256)
            stat_chunk(w_up[0], FF + st * 256)
        C_DN = len(chunks)
        for j in range(FT // 2):
            chunks.append(("d", w_down[0][j * 256:(j + 1) * 256, :].rearrange("(k p) n -> p k n", p=P)))
        C_IN1 = len(chunks)
        wc = w_in_c[0]
        for i in range(8):
            stat_chunk(wc, i * 256)
        for nh in range(2):
            for kh in range(2):
                move_chunk(wc, 2048 + nh * 512, kh)
        C_OUT1 = len(chunks)
        for nh in range(2):
            for kh in range(2):
                move_chunk(w_out_c[0], nh * 512, kh)
        C_MOE = len(chunks)
        NST = EFT // 4
        CPI = 6 * NST
        assert CPI % MRING == 0 and CPI % MSPLIT == 0 and N_MOD % RING == 0

        loads = []
        m_next = N_MOD
        for c in range(C_MOE):
            loads.append(("weight", c))
            rows_here = {C_OUT0: MOD_ATT, C_UP: MOD_GAP, C_IN1: MOD_GAP}.get(c, 0)
            for _ in range(2 * rows_here):
                loads.append(("mod", m_next))
                m_next += 1
        assert m_next == DEPTH * N_MOD
        pos = {("mod", m): m for m in range(N_MOD)}
        pos.update({key: N_MOD + i for i, key in enumerate(loads)})

        def raw(kind, c):
            return RAW[:, pos[kind, c] % RING, :]

        def landed(kind, c):
            return s_landed[pos[kind, c] % RING], 16 * (pos[kind, c] // RING + 1)

        def kview(kind, t):
            k = {"s": 8, "m": 4, "d": 2}[kind]
            return t.rearrange("p (k n) -> p k n", k=k)

        s_const = sem("constants_landed")
        s_x = sem("x_landed")
        s_small = sem("small_inputs_landed")
        s_wr = sem("router_weights_landed")
        s_landed = [sem(f"raw_landed{i}") for i in range(RING)]
        s_mland = [sem(f"expert_raw_landed{i}") for i in range(MRING)]
        s_sth = sem("silu_c_hi_ready")
        s_stl = sem("silu_c_split")
        s_mhi = sem("mod_weights_hi_ready")
        s_mlo = sem("mod_weights_split")
        s_modused = sem("mod_chunk_used")
        s_hi = sem("weights_hi_ready")
        s_lo = sem("weights_lo_ready")
        s_khalf = sem("first_contraction_half_used")
        s_vt = sem("vectors_transposed")
        s_vtc = sem("vectors_copied")
        s_silu = sem("silu_c_ready")
        s_modrow = sem("mod_row_copied")
        s_modcol = sem("mod_columns_in_psum")
        s_modc = sem("mod_columns_ready")
        s_zero = sem("zero_tile_ready")
        s_zp = sem("bias_pad_zeroed")
        s_zpl = sem("bias_pad_landed")
        s_fb = sem("bias_rows_stored")
        s_bl = sem("bias_landed")
        s_hps = sem("h_transposed")
        s_hf = sem("h_modulated")
        s_hr = sem("h_split")
        s_qps = sem("projection_in_psum")
        s_qdr = sem("projection_copied")
        s_rps = sem("rotated_in_psum")
        s_rope = sem("rope_done")
        s_sc = sem("scores_in_psum")
        s_scd = sem("scores_copied")
        s_nm = sem("negative_max_ready")
        s_sink = sem("sink_exp_done")
        s_exp = sem("exp_done")
        s_cmb = sem("difference_ready")
        s_ptp = sem("probs_transposed")
        s_ptc = sem("probs_transposed_copied")
        s_ops = sem("attention_in_psum")
        s_osb = sem("attention_copied")
        s_ob = sem("attention_block_ready")
        s_otp = sem("attention_block_transposed")
        s_oth = sem("attention_hi_ready")
        s_otr = sem("attention_split")
        s_ssq = sem("square_sums_ready")
        s_ssr = sem("square_sums_rooted")
        s_gps = sem("gate_rows_in_psum")
        s_gate = sem("gate_rows_ready")
        s_lnr = sem("norm_rows_landed")
        s_yps = sem("sublayer_out_in_psum")
        s_yread = sem("sublayer_out_read")
        s_var = sem("variance_ready")
        s_std = sem("deviation_ready")
        s_rs = sem("norm_scale_ready")
        s_xh = sem("normalised_block")
        s_ln = sem("norm_block_done")
        s_up = sem("up_in_psum")
        s_silg = sem("ffn_silu_done")
        s_mul = sem("ffn_product_done")
        s_gh = sem("ffn_hi_ready")
        s_gl = sem("ffn_lo_ready")
        s_dn = sem("ffn_down_chunk_done")
        s_cm = sem("item_constants_landed")
        s_lg = sem("router_logits_in_psum")
        s_gx = sem("router_exp_input")
        s_ge = sem("router_exp_done")
        s_rm = sem("routing_mask_ready")
        s_rk = sem("ranks_and_counts_in_psum")
        s_pr = sem("item_presence_ready")
        s_ix = sem("item_numbers_in_psum")
        s_isel = sem("item_selection_ready")
        s_tb = sem("item_table_in_psum")
        s_tab = sem("item_table_ready")
        s_sel = sem("item_token_selection_ready")
        s_gat = sem("gathered_in_psum")
        s_gev = sem("gathered_modulated")
        s_he = sem("gathered_split")
        s_mup = sem("expert_up_chunk_done")
        s_msil = sem("expert_silu_done")
        s_mrd = sem("expert_product_ready")
        s_tp = sem("expert_product_transposed")
        s_th = sem("expert_product_hi_ready")
        s_at = sem("expert_product_split")
        s_mdn = sem("expert_down_chunk_done")
        s_y0 = sem("expert_out_banks_cleared")
        s_y = sem("expert_out_copied")
        s_sc2 = sem("scattered_in_psum")
        s_gtp = sem("return_matrix_in_psum")
        s_gtc = sem("return_matrix_ready")
        s_ini = sem("expert_buffers_cleared")
        s_myd = sem("expert_out_added")
        s_dve2 = sem("vector_chain_after_experts")
        s_out = sem("output_stored")
        s_lam = sem("lambda_exp_input")
        s_lame = sem("lambda_exp_done")
        s_dve = sem("vector_chain")

        groups = [[(b, g) for b in range(4) for g in range(4)], [(b, g) for b in (2, 3) for g in range(4)]]
        NG0 = len(groups[0])
        assert 2 * MOD_ATT == NG0 and MOD_ATT + 2 * MOD_GAP == NB_MOD
        g_base = [0, NG0]
        pt_base = [0, 4 * NG0]
        NPT = 4 * NG0 + 2 * len(groups[1])

        def n_keys(l, b):
            return CTX if l == 0 and b < 2 else TOK

        def pts_before(gi):
            return 4 * gi if gi <= NG0 else 4 * NG0 + 2 * (gi - NG0)

        turn_banks = (6, 5)

        def ln_blocks(p):
            return (0, 1, 2, 3) if p < 2 else (2, 3)

        ln_before = [0, 4, 8, 10, 12]
        y_read = [0, 8, 16, 20]
        y_before = [0, 8, 8, 12]
        NT0 = 4 + 1 + 4 + 4 + 4 + 4
        NT1 = 8 + 8 + 8

        def head_of(l, g, j):
            if l == 1:
                return 2 * g + j // 2, j % 2, 2 * g + j // 2
            if g < 2:
                h = 4 * g + j
                return h // 2, h % 2, g
            h = 4 * (g - 2) + j
            return 4 + h // 2, h % 2, 2 + h // 2

        def score_bank(l, u):
            return u % 2 if l == 0 else (0, 1, 7)[u % 3]

        def values(l, g, j):
            if l == 1:
                return V1[:, :, (2 * g + j) * P:(2 * g + j + 1) * P]
            if g < 2:
                return V0[:, :, g * HD:(g + 1) * HD]
            h = 4 * (g - 2) + j
            return V0[:, :, P + h * HD:P + (h + 1) * HD]

        PB = 6

        def tile_bank(l, t):
            return (t - (0 if l == 0 else NT0) + 4) % PB

        def rope_tiles(l, i):
            if l == 0:
                tiles = {0: [(QT, 0), (QT, 1)], 1: [(QT, 2), (QT, 3)], 2: [(KTT, 0), (KTT, 1)]}.get(i, [])
                return [(2 * i + j, *t) for j, t in enumerate(tiles)]
            if i >= 8:
                return []
            return [(N_ROPE0 + 2 * i + j, QT if i < 4 else KTT, 2 * (i % 4) + j) for j in range(2)]

        N_ROPE0, N_ROPE = 6, 6 + 16

        def projection(l):
            every, lat = slice(0, TOK), slice(CTX, TOK)
            plan = []
            if l == 0:
                for i in range(2):
                    plan.append([(every, QT[:, 2 * i + j, :]) for j in range(2)])
                plan.append([(every, "keys of A")] + [(slice(P, 2 * P), V0[:, b, 0:P]) for b in range(BLK)])
                for i in range(2):
                    plan.append([(every, QT[:, 4 + 2 * i + j, :]) for j in range(2)])
                for i in range(2):
                    plan.append([(every, KTT[:, 2 + 2 * i + j, :]) for j in range(2)])
                plan += [[], [(every, V0[:, b, P:P + 512]) for b in range(BLK)]]
            else:
                for i in range(4):
                    plan.append([(slice(0, SEQ), QT[:, 2 * i + j, lat]) for j in range(2)])
                for i in range(4):
                    plan.append([(every, KTT[:, 2 * i + j, :]) for j in range(2)])
                for nh in range(2):
                    plan += [[], [(every, V1[:, b, nh * 512:(nh + 1) * 512]) for b in range(BLK)]]
            c0 = 0 if l == 0 else C_IN1
            return [(c0 + i, tiles) for i, tiles in enumerate(plan)]

        used = []
        t, kh_n, y_n = 0, 0, 0
        for l in range(2):
            for c, tiles in projection(l):
                t += len(tiles)
                kh_n += not tiles
                used.append((s_qps, t) if tiles else (s_khalf, kh_n))
            for nh in range(2):
                kh_n += 1
                y_n += len(ln_blocks(2 * l))
                used += [(s_khalf, kh_n), (s_yps, y_n)]
            if l == 0:
                used += [(s_up, 2 * i + 2) for i in range(FT)]
                used += [(s_dn, j + 1 + (j == FT // 2 - 1)) for j in range(FT // 2)]
        assert len(used) == C_MOE and t == NT0 + NT1

        block = ctx.enter_context(nc.Block())

        order = [(w, 0, h) for w in "gu" for h in range(2)]
        for st in range(1, NST):
            order += [(w, st, h) for w in "gu" for h in range(2)] + [("d", st - 1, h) for h in range(2)]
        order += [("d", NST - 1, h) for h in range(2)]

        GATHER = [("g", NST - 2, 0), ("d", NST - 2, 1)]

        def place(what, st, half):
            return order.index((what, st, half))

        def up_done(i, what, st, half):
            return i * (4 * NST) + (4 * st + 2 * (what == "u") + half + 1)

        def down_done(i, st, half):
            return i * (2 * NST) + (2 * st + half + 4)

        def item_used(q, i):
            if q < MSPLIT:
                return s_mdn, i * (2 * NST) + (q + 1)
            what, st, half = order[q - MSPLIT]
            return (s_mdn, down_done(i, st, half)) if what == "d" else (s_mup, up_done(i, what, st, half))

        def expert_raw(q):
            slot = q % MRING
            return RAW[:, slot, :] if slot < RING else RAWX[:, slot - RING, :]

        def expert_split(q):
            slot = q % MSPLIT
            return (WH[:, slot, :], WL[:, slot, :]) if slot < 2 else (WHX[:, :], WLX[:, :])

        def count_load(eng):
            eng.wait_ge(s_tab, 1)
            return eng.value_load(TAB[0:1, 0:1], min_val=1, max_val=2 * NE)

        def behind(what, st):
            if what == "silu":
                return place("g", st, 1) + MSPLIT
            if what == "mul":
                return place("u", st, 1) + MSPLIT
            return place("g", st + 1, 1) + MSPLIT if st + 1 < NST else place("d", NST - 2, 0) + MSPLIT

        @block.sync
        def _(sp):
            sp.dma_start(VR[:, :], vecs).then_inc(s_const, 16)
            sp.dma_start(CN[:, :], consts).then_inc(s_const, 16)
            wm = w_mod.rearrange("l (kh k p) n -> l kh p k n", kh=2, p=P)

            def load_mod(m):
                l, nb, kh = m // N_MOD, m // 2 % NB_MOD, m % 2
                sp.dma_start(kview("m", raw("mod", m)), wm[l, kh][:, :, nb * 512:(nb + 1) * 512])\
                    .then_inc(landed("mod", m)[0], 16)

            for c in range(N_MOD):
                if c >= RING:
                    sp.wait_ge(s_mlo, c - RING + 1)
                load_mod(c)
            order_of = {v: k for k, v in pos.items()}
            for what, c in loads:
                before, cb = order_of[pos[what, c] - RING]
                sp.wait_ge(s_lo if before == "weight" else s_mlo if cb < N_MOD else s_modused, cb + 1)
                if what == "mod":
                    load_mod(c)
                else:
                    kind, src = chunks[c]
                    sp.dma_start(kview(kind, raw(what, c)), src).then_inc(landed(what, c)[0], 16)
            sp.wait_ge(s_lo, C_MOE)
            up = w_eup[0].rearrange("e (k p) n -> p e k n", p=P)
            dn = w_edown[0].rearrange("e (k p) n -> p e k n", p=P)
            n_items = count_load(sp)
            with sp.Fori(0, n_items) as i:
                e = sp.value_load(TAB[0:1, bass.ds(i + 24, 1)], min_val=0, max_val=NE - 1)
                for q, (what, st, half) in enumerate(order):
                    sp.wait_ge(s_lo, i * CPI + (C_MOE - MRING + q + 1))
                    if what == "d":
                        k0 = st * 4 + half * 2
                        src, kind = dn[:, bass.ds(e, 1), k0:k0 + 2, :], "d"
                    else:
                        n0 = st * 512 + (EFF if what == "u" else 0)
                        src, kind = up[:, bass.ds(e, 1), half * 4:half * 4 + 4, n0:n0 + 512], "m"
                    sp.dma_start(kview(kind, expert_raw(q)), src.rearrange("p e k n -> p (e k) n"))\
                        .then_inc(s_mland[q % MRING], 16)
            for b in (2, 3):
                sp.wait_ge(s_ln, ln_before[3] + b - 1)
                sp.dma_start(out[0, (b - 2) * P:(b - 1) * P, :], X[:, b, :]).then_inc(s_out, 16)
            sp.wait_ge(s_out, 32)

        @block.gpsimd
        def _(gp):
            gp.memset(ZP[:, :], 0.0).then_inc(s_zp, 1)
            gp.memset(ZERO[:, :], 0.0).then_inc(s_zero, 1)
            for b in range(2):
                gp.dma_start(X[:, b, :], ctx_in[0, b * P:(b + 1) * P, :]).then_inc(s_x, 16)
                gp.dma_start(X[:, 2 + b, :], x[0, b * P:(b + 1) * P, :]).then_inc(s_x, 16)
            gp.dma_start(SINK[:, :], sink_a[0].partition_broadcast(P)).then_inc(s_small, 16)
            gp.dma_start(LAMP[:, :], lam_c[0].rearrange("a b -> (a b)").partition_broadcast(P)).then_inc(s_small, 16)
            gp.dma_start(SUBL[:, :], subln[0].partition_broadcast(P)).then_inc(s_small, 16)
            gp.wait_ge(s_zp, 1)
            for h in range(B_HEADS):
                gp.dma_start(ZP[h * DR:(h + 1) * DR, GRID_W - NKW:GRID_W - NKW + DC],
                             rpb[0, h, KH_MAX - ROWS:KH_MAX - ROWS + DR]).then_inc(s_zpl, 16)
            gp.wait_ge(s_zpl, 16 * B_HEADS)
            gp.wait_ge(s_modused, N_MOD)
            rows = ZP[:, 0:ZL]
            gp.dma_start(fbias, rows.unsqueeze(1).to_broadcast([B_HEADS * DR, GRID_W, ZL])).then_inc(s_fb, 16)
            gp.wait_ge(s_fb, 16)
            fb = fbias.rearrange("(h r) c z -> r h (c z)", h=B_HEADS)
            for r in range(ROWS):
                for kr in range(ROWS):
                    src = fb[kr - r + ROWS - 1][:, GRID_W - 1:GRID_W - 1 + GRID_W * (ZL - 1)]
                    src = src.rearrange("h (c y) -> c h y", y=ZL - 1)[:, :, 0:GRID_W]
                    p0 = (r % 2) * GRID_W
                    gp.dma_start(BIAS[p0:p0 + GRID_W, r // 2, :, kr * GRID_W:(kr + 1) * GRID_W], src)\
                        .then_inc(s_bl, 16)
            for p in range(4):
                if p % 2 == 0:
                    gp.wait_ge(s_otr, 4 if p == 0 else 6)
                else:
                    gp.wait_ge(s_ln, ln_before[p])
                gp.dma_start(LNR[:, 0, :], ln_g[p // 2, p % 2].partition_broadcast(P)).then_inc(s_lnr, 16)
                gp.dma_start(LNR[:, 1, :], ln_b[p // 2, p % 2].partition_broadcast(P)).then_inc(s_lnr, 16)
                if p == 2:
                    gp.dma_start(CM[:, :], item_consts).then_inc(s_cm, 16)
                    gp.dma_start(WR[:, :, :], w_router[0].rearrange("(k p) e -> p k e", p=P)).then_inc(s_wr, 16)

        @block.tensor
        def _(pe):
            mm = nc.tensor.matmul

            def mm3(ps, ah, al, bh, bl, start, stop):
                mm(ps, ah, bh, start=start, stop=False)
                mm(ps, ah, bl, start=False, stop=False)
                return mm(ps, al, bh, start=False, stop=stop)

            pe.wait_ge(s_const, 32)
            nc.tensor.transpose(PS[:, 7, 0:112], VR[:, :], CN[0:112, C_ID:C_ID + 112]).then_inc(s_vt, 1)

            def mod_columns(n, bank):
                pe.wait_ge(s_modrow, n + 1)
                for j in range(4):
                    at = (n % NB_MOD * 4 + j) * 2
                    row, add = (mod_row(n, 4), CN[0:4, C_ADD:C_ADD + 2]) if n < NB_MOD else \
                        (mod_row(n), CN[0:2, C_ID:C_ID + 2])
                    last = mm(PS[:, bank, at:at + 2], row[:, j, :], add, start=True, stop=True)
                return last

            def mod_half(n, kh, ps):
                pe.wait_ge(*landed("mod", 2 * n + kh))
                w = kview("m", raw("mod", 2 * n + kh))
                for k in range(4):
                    last = mm(ps, ST[:, kh * 4 + k, :], w[:, k, :],
                              start=(kh == 0 and k == 0), stop=(kh == 1 and k == 3))
                last.then_inc(s_modused, 1)

            def mod_half_split(n, kh, bank):
                m = 2 * n + kh
                pe.wait_ge(s_mlo, m + 1)
                wh, wl = kview("m", WH[:, m % 2, :]), kview("m", WL[:, m % 2, :])
                for k in range(4):
                    kt = kh * 4 + k
                    mm(PS[0:4, bank, :], STS[:, kt, :], wh[:, k, :], start=(kt == 0), stop=False)
                    last = mm(PS[0:4, bank, :], STS[:, kt, :], wl[:, k, :], start=False, stop=(kt == KT - 1))
                last.then_inc(s_modused, 1)

            def mod_rows(n0, n1, bank):
                for n in range(n0, n1):
                    if n - n0 >= 2:
                        pe.wait_ge(s_modrow, n - 1)
                    for kh in range(2):
                        if n < NB_MOD:
                            mod_half_split(n, kh, n % 2)
                        else:
                            mod_half(n, kh, PS[0:2, n % 2, :])
                    if n > n0:
                        mod_columns(n - 1, bank)
                mod_columns(n1 - 1, bank).then_inc(s_modcol, 1)

            def mod_gap(p):
                pe.wait_ge(s_yread, 8 * p + 4)
                n0 = NB_MOD + MOD_ATT + p * MOD_GAP
                mod_rows(n0, n0 + MOD_GAP, 3)

            pe.wait_ge(s_stl, 1)
            mod_rows(0, NB_MOD, 2)

            def h_phase(h):
                bs = ln_blocks(h) if h == 3 else (0, 1, 2, 3)
                if h == 0:
                    pe.wait_ge(s_x, 64)
                    pe.wait_ge(s_modc, 1)
                else:
                    pe.wait_ge(s_ln, ln_before[h])
                for dt in range(KT):
                    if dt >= 4:
                        pe.wait_ge(s_hf, 8 * h + dt - 3)
                    if dt == 3 and h in (1, 2):
                        pe.wait_ge(s_modc, 1 + MOD_ATT + h)
                    for b in bs:
                        last = nc.tensor.transpose(PS[:, dt % 4, b * P:(b + 1) * P],
                                                   X[:, b, dt * P:(dt + 1) * P], ident)
                    last.then_inc(s_hps, 1)

            def gates(p):
                l, seg = p // 2, 2 if p % 2 == 0 else 5
                for s, st in ((0, 1), (1, 0)) if l == 0 else ((1, 0),):
                    for half in range(2):
                        for j in range(4):
                            col = MODC[:, l, seg * 8 + half * 4 + j, st:st + 1].to_broadcast([P, P])
                            last = mm(PS[:, 4 + s * 2 + half, j * P:(j + 1) * P], col, ident,
                                      start=True, stop=True)
                        last.then_inc(s_gps, 1)

            def split_ready(c):
                pe.wait_ge(s_lo, c + 1)
                return c % 2

            def rope(l, i, tiles):
                for n, tt, j in rope_tiles(l, i):
                    pe.wait_ge(s_qdr, tiles)
                    if n >= 2:
                        pe.wait_ge(s_rope, n - 1)
                    mm(PS[:, 6 + n % 2, 0:SEQ], CN[:, C_ROT:C_ROT + P], tt[:, j, CTX:TOK],
                       start=True, stop=True).then_inc(s_rps, 1)

            def project(l):
                t0 = 0 if l == 0 else NT0
                c = c0 = 0 if l == 0 else C_IN1
                t = [t0]

                def tile(n, fill):
                    if t[0] - t0 >= PB:
                        pe.wait_ge(s_qdr, t[0] - PB + 1)
                    fill(PS[:, tile_bank(l, t[0]), 0:n]).then_inc(s_qps, 1)
                    t[0] += 1

                def standing(w, cols, toks):
                    def fill(ps):
                        for k in range(KT):
                            if t[0] == t0:
                                pe.wait_ge(s_hr, 16 * l + k + 1)
                            last = mm3(ps, cols(WH, w, k), cols(WL, w, k), HH[:, k, toks], HL[:, k, toks],
                                       k == 0, k == KT - 1)
                        return last
                    return fill

                def plain(n0):
                    return lambda W, w, k: kview("s", W[:, w, :])[:, k, n0:n0 + P]

                every, lat = slice(0, TOK), slice(CTX, TOK)
                if l == 0:
                    plan = ["q", "q", "a", "q", "q", "k", "k"]
                else:
                    plan = ["q"] * 4 + ["k"] * 4
                for kind in plan:
                    w = split_ready(c)
                    if kind == "a":
                        tile(TOK, standing(w, plain(0), every))
                        for b in range(BLK):
                            def fill(ps, b=b):
                                for k in range(KT):
                                    tk = slice(b * P, (b + 1) * P)
                                    last = mm3(ps, HH[:, k, tk], HL[:, k, tk], kview("s", WH[:, w, :])[:, k, :],
                                               kview("s", WL[:, w, :])[:, k, :], k == 0, k == KT - 1)
                                return last
                            tile(256, fill)
                    else:
                        toks = lat if (l == 1 and kind == "q") else every
                        for j in range(2):
                            tile(toks.stop - toks.start, standing(w, plain(j * P), toks))
                    if c > c0:
                        rope(l, c - c0 - 1, drained)
                    drained = t[0]
                    c += 1
                rope(l, c - c0 - 1, drained)
                for nh in range(1 if l == 0 else 2):
                    for b in range(BLK):
                        if t[0] + b - t0 >= PB:
                            pe.wait_ge(s_qdr, t[0] + b - PB + 1)
                    for kh in range(2):
                        w = split_ready(c)
                        for b in range(BLK):
                            for k in range(4):
                                tk = slice(b * P, (b + 1) * P)
                                last = mm3(PS[:, tile_bank(l, t[0] + b), :], HH[:, kh * 4 + k, tk], HL[:, kh * 4 + k, tk],
                                           kview("m", WH[:, w, :])[:, k, :], kview("m", WL[:, w, :])[:, k, :],
                                           kh == 0 and k == 0, kh == 1 and k == 3)
                            if kh == 1:
                                last.then_inc(s_qps, 1)
                        if kh == 0:
                            last.then_inc(s_khalf, 1)
                        c += 1
                    t[0] += BLK

            def attention(l):
                gs = groups[l]
                pe.wait_ge(s_qdr, NT0 if l == 0 else NT0 + NT1)
                pe.wait_ge(s_rope, N_ROPE0 if l == 0 else N_ROPE)

                def scores(gi, b, g, units):
                    nk = n_keys(l, b)
                    for j in units:
                        u = 4 * gi + j
                        if l == 0 and u >= 2:
                            pe.wait_ge(s_scd, u - 1)
                        if l == 1 and u - 4 * g_base[l] >= 3:
                            pe.wait_ge(s_exp, u - 2)
                        qt, half, kt = head_of(l, g, j)
                        hp = slice(half * HD, half * HD + HD)
                        mm(PS[:, score_bank(l, u), 0:nk], QT[hp, qt, b * P:(b + 1) * P], KTT[hp, kt, 0:nk],
                           start=True, stop=True).then_inc(s_sc, 1)

                def weigh(gi, b, g):
                    nk = n_keys(l, b)
                    units = 4 if l == 0 else 2
                    n0 = pts_before(gi)

                    def turn(j):
                        n = n0 + j
                        if l == 0:
                            pe.wait_ge(s_exp, 4 * gi + j + 1)
                        else:
                            pe.wait_ge(s_cmb, 2 * (gi - NG0) + j + 1)
                        if n >= 2:
                            pe.wait_ge(s_ptc, n - 1)
                        for kt in range(nk // P):
                            last = nc.tensor.transpose(PS[:, 2 + n % 2, kt * P:(kt + 1) * P],
                                                       S[:, gi % 2, j if l == 0 else 2 * j, kt * P:(kt + 1) * P],
                                                       ident)
                        last.then_inc(s_ptp, 1)

                    turn(0)
                    for j in range(units):
                        if j + 1 < units:
                            turn(j + 1)
                        if j == 0 and gi >= 2:
                            pe.wait_ge(s_osb, gi - 1)
                        if j == 0 and gi % 4 == 1 and gi >= 4:
                            pe.wait_ge(s_otr, gi // 4)
                        pe.wait_ge(s_ptc, n0 + j + 1)
                        n = HD if l == 0 else P
                        for kt in range(nk // P):
                            last = mm(PS[:, 4 + gi % 2, j * n:(j + 1) * n], PT[:, (n0 + j) % 2, kt * P:(kt + 1) * P],
                                      values(l, g, j)[:, kt, :], start=(kt == 0), stop=(kt == nk // P - 1))
                    last.then_inc(s_ops, 1)

                def turn_block(i):
                    n = i + (0 if l == 0 else 4)
                    if l == 0:
                        pe.wait_ge(s_osb, 4 * (i + 1))
                    else:
                        pe.wait_ge(s_ob, i + 1)
                    if n >= 1:
                        pe.wait_ge(s_otr, n)
                    if l == 0:
                        pe.wait_ge(s_modc, 1 + 2 * i + 1)
                    for half in range(2):
                        for j in range(4):
                            last = nc.tensor.transpose(PS[:, turn_banks[half], j * P:(j + 1) * P],
                                                       OSB[:, (half * 4 + j) * P:(half * 4 + j + 1) * P], ident)
                    last.then_inc(s_otp, 1)

                def mod_between(i):
                    if i % 2 == 0 and i >= 2:
                        if i >= 4:
                            pe.wait_ge(s_otr, i // 4)
                            pe.wait_ge(s_modc, i // 2)
                        mod_columns(NB_MOD + i // 2 - 1, 6).then_inc(s_modcol, 1)
                    mod_half(NB_MOD + i // 2, i % 2, PS[0:2, 7, :])

                scores(g_base[l], *gs[0], range(4))
                for i, (b, g) in enumerate(gs):
                    gi = g_base[l] + i
                    if i + 1 < len(gs):
                        scores(gi + 1, *gs[i + 1], (0, 1))
                    if l == 0:
                        mod_between(i)
                    if i + 1 < len(gs):
                        scores(gi + 1, *gs[i + 1], (2, 3))
                    weigh(gi, b, g)
                    if i == NG0 - 1:
                        mod_columns(NB_MOD + i // 2, 7).then_inc(s_modcol, 1)
                    if g == 3:
                        turn_block(i // 4)

            def project_out(l):
                c = C_OUT0 if l == 0 else C_OUT1
                pe.wait_ge(s_otr, 4 if l == 0 else 6)
                gates(2 * l)
                for nh in range(2):
                    if nh == 1:
                        pe.wait_ge(s_gate, 4 if l == 0 else 10)
                        if l == 0:
                            pe.wait_ge(s_modc, 1 + MOD_ATT)
                    for kh in range(2):
                        w = split_ready(c)
                        for b in ln_blocks(2 * l):
                            tk = slice(b * P, (b + 1) * P)
                            for k in range(4):
                                last = mm3(PS[:, nh * 4 + b, :], HH[:, kh * 4 + k, tk], HL[:, kh * 4 + k, tk],
                                           kview("m", WH[:, w, :])[:, k, :], kview("m", WL[:, w, :])[:, k, :],
                                           kh == 0 and k == 0, kh == 1 and k == 3)
                            if kh == 1:
                                last.then_inc(s_yps, 1)
                        if kh == 0:
                            last.then_inc(s_khalf, 1)
                        c += 1

            def ffn():
                pe.wait_ge(s_hf, 16)
                gates(1)
                c = C_UP
                for st in range(FT // 2):
                    if st == 1:
                        pe.wait_ge(s_gate, 8)
                    if st >= 2:
                        pe.wait_ge(s_mul, 2 * (st - 1))
                    for gu in range(2):
                        w = split_ready(c)
                        for j in range(2):
                            for k in range(KT):
                                if (st, gu, j) == (0, 0, 0):
                                    pe.wait_ge(s_hr, 8 + k + 1)
                                last = mm3(PS[:, st % 2 * 4 + gu * 2 + j, :],
                                           kview("s", WH[:, w, :])[:, k, j * P:(j + 1) * P],
                                           kview("s", WL[:, w, :])[:, k, j * P:(j + 1) * P],
                                           HH[:, k, :], HL[:, k, :], k == 0, k == KT - 1)
                            last.then_inc(s_up, 1)
                        c += 1
                pe.wait_ge(s_mul, FT)
                for j in range(FT // 2):
                    w = split_ready(c)
                    pe.wait_ge(s_gl, j + 1)
                    for nh in range(2):
                        for b in range(BLK):
                            tk = slice(b * P, (b + 1) * P)
                            for k in range(2):
                                last = mm3(PS[:, nh * 4 + b, :], GH[:, j % 2, k, tk], GL[:, j % 2, k, tk],
                                           kview("d", WH[:, w, :])[:, k, nh * 512:(nh + 1) * 512],
                                           kview("d", WL[:, w, :])[:, k, nh * 512:(nh + 1) * 512],
                                           j == 0 and k == 0, j == FT // 2 - 1 and k == 1)
                        if nh == 1 or j == FT // 2 - 1:
                            last.then_inc(s_dn, 1)
                    c += 1

            def router():
                pe.wait_ge(s_hf, 32)
                pe.wait_ge(s_wr, 16)
                pe.wait_ge(s_cm, 16)
                for i in range(2):
                    for k in range(KT):
                        last = mm(PS[:, i, 0:NE], F[:, k, (2 + i) * P:(3 + i) * P], WR[:, k, :],
                                  start=(k == 0), stop=(k == KT - 1))
                    last.then_inc(s_lg, 1)
                gates(3)
                tri, one = CM[:, M_TRI:M_TRI + P], CM[:, M_ONE:M_ONE + P]
                pe.wait_ge(s_rm, 1)
                mm(PS[:, 2, 0:8], tri, MASKS[:, 0, :], start=True, stop=True)
                mm(PS[:, 2, 8:16], tri, MASKS[:, 1, :], start=True, stop=False)
                mm(PS[:, 2, 8:16], one, MASKS[:, 0, :], start=False, stop=True)
                for b in range(2):
                    last = mm(PS[0:16, 3, 0:1], MASK2[:, b, :], one[:, 0:1], start=(b == 0), stop=(b == 1))
                last.then_inc(s_rk, 1)
                pe.wait_ge(s_pr, 1)
                mm(PS[0:16, 3, 8:9], tri[0:16, 0:16], PRES, start=True, stop=True)
                mm(PS[0:1, 3, 16:17], PRES, one[0:16, 0:1], start=True, stop=True).then_inc(s_ix, 1)
                pe.wait_ge(s_isel, 1)
                mm(PS[0:1, 3, 24:40], CM[0:16, M_C:M_C + 1], ISEL, start=True, stop=True)
                mm(PS[0:1, 3, 40:56], CM[0:16, M_E:M_E + 1], ISEL, start=True, stop=True).then_inc(s_tb, 1)
                pe.wait_ge(s_gate, 12)

            def gather(half):
                for j in range(4):
                    dt = half * 4 + j
                    for b in range(2):
                        last = mm(PS[:, 7, j * P:(j + 1) * P], X[:, 2 + b, dt * P:(dt + 1) * P],
                                  SEL[:, b, :], start=(b == 0), stop=(b == 1))
                last.then_inc(s_gat, 1)

            def scatter(i, parts):
                for part in parts:
                    b, nh = divmod(part, 2)
                    if part >= 2:
                        pe.wait_ge(s_myd, i * 4 + (part - 1))
                    mm(PS[:, 7 - part % 2, :], BACK[:, b * P:(b + 1) * P], Y[:, nh, :],
                       start=True, stop=True).then_inc(s_sc2, 1)

            def turn(i, st):
                pe.wait_ge(s_mrd, i * NST + (st + 2))
                if st == 0:
                    pe.wait_ge(s_myd, i * 4 + 4)
                else:
                    pe.wait_ge(s_at, i * NST + st)
                for j in range(4):
                    last = nc.tensor.transpose(PS[:, 6, j * P:(j + 1) * P], AF[:, st % 2, j * P:(j + 1) * P],
                                               ident)
                last.then_inc(s_tp, 1)

            def experts():
                mm(PS[:, 4, :], ZERO[:, 0:P], ZERO[:, :], start=True, stop=True)
                mm(PS[:, 5, :], ZERO[:, 0:P], ZERO[:, :], start=True, stop=True).then_inc(s_y0, 1)
                pe.wait_ge(s_tab, 1)
                pe.wait_ge(s_sel, 1)
                gather(0)
                pe.wait_ge(s_gev, 1)
                gather(1)
                pe.wait_ge(s_ini, 1)
                n_items = count_load(pe)
                with pe.Fori(0, n_items) as i:
                    pe.wait_ge(s_he, i + 1)
                    for q, (what, st, half) in enumerate(order):
                        pe.wait_ge(s_lo, i * CPI + (C_MOE + q + 1))
                        wh, wl = expert_split(q)
                        if what == "d":
                            if half == 0:
                                pe.wait_ge(s_at, i * NST + (st + 1))
                            if st == 0 and half == 0:
                                pe.wait_ge(s_y, i * 2 + 2)
                            for k in range(2):
                                tk = slice((half * 2 + k) * P, (half * 2 + k + 1) * P)
                                for nh in range(2):
                                    last = mm3(PS[:, 4 + nh, :], TH[:, st % 2, tk], TL[:, st % 2, tk],
                                               kview("d", wh)[:, k, nh * 512:(nh + 1) * 512],
                                               kview("d", wl)[:, k, nh * 512:(nh + 1) * 512],
                                               st == 0 and half == 0 and k == 0,
                                               st == NST - 1 and half == 1 and k == 1)
                            last.then_inc(s_mdn, 1)
                        else:
                            if what == "g" and half == 0:
                                pe.wait_ge(s_mrd, i * NST + max(st, 1))
                            bank = st % 2 * 2 + (what == "u")
                            for k in range(4):
                                kt = half * 4 + k
                                last = mm3(PS[:, bank, :], HE[:, kt, :], LE[:, kt, :], kview("m", wh)[:, k, :],
                                           kview("m", wl)[:, k, :], kt == 0, kt == KT - 1)
                            last.then_inc(s_mup, 1)
                        if (what, st, half) == ("u", 0, 0):
                            pe.wait_ge(s_y, i * 2 + 2)
                            pe.wait_ge(s_gev, i * 2 + 2)
                            scatter(i, (0, 1))
                        elif (what, st, half) == ("g", 1, 0):
                            scatter(i, (2, 3))
                        elif what == "g" and half == 1 and st >= 1:
                            if st == 1:
                                pe.wait_ge(s_myd, i * 4 + 3)
                                for b in range(2):
                                    last = nc.tensor.transpose(PS[:, 7, b * P:(b + 1) * P], SELG[:, b, :], ident)
                                last.then_inc(s_gtp, 1)
                            turn(i, st - 1)
                        elif (what, st, half) == GATHER[0]:
                            pe.wait_ge(s_gtc, i + 1)
                            pe.wait_ge(s_sel, i + 2)
                            gather(0)
                        elif (what, st, half) == GATHER[1]:
                            turn(i, NST - 1)
                            pe.wait_ge(s_gev, i * 2 + 3)
                            gather(1)
                pe.wait_ge(s_y, n_items * 2 + 2)
                pe.wait_ge(s_gev, n_items * 2 + 2)
                pe.wait_ge(s_gtc, n_items)
                scatter(n_items, range(4))

            h_phase(0)
            project(0)
            attention(0)
            project_out(0)
            mod_gap(0)
            h_phase(1)
            ffn()
            mod_gap(1)
            h_phase(2)
            project(1)
            attention(1)
            project_out(1)
            h_phase(3)
            router()
            experts()

        @block.scalar
        def _(act):
            fn = nc.scalar.activation
            done = [0]

            def split(upto):
                for c in range(done[0], min(upto, C_MOE)):
                    act.wait_ge(*landed("weight", c))
                    if c >= 2:
                        act.wait_ge(*used[c - 2])
                    else:
                        act.wait_ge(s_modused, N_MOD - 1 + c)
                    fn(WH[:, c % 2, :], raw("weight", c), ACT.Copy).then_inc(s_hi, 1)
                    done[0] = c + 1

            act.wait_ge(s_vtc, 1)
            for s in range(2):
                fn(ST[:, :, s], VT[:, 96 + 8 * s:104 + 8 * s], ACT.Silu).then_inc(s_silu, 1)
            act.wait_ge(s_silu, 2)
            fn(STS[:, :, 0:2], ST[:, :, :], ACT.Copy).then_inc(s_sth, 1)

            def mod_row_out(n, bank):
                act.wait_ge(s_modused, 2 * n + 2)
                parts = 4 if n < NB_MOD else 2
                fn(mod_row(n, parts), PS[0:parts, bank, :].rearrange("p (j q) -> p j q", j=4), ACT.Copy)\
                    .then_inc(s_modrow, 1)

            for m in range(N_MOD):
                act.wait_ge(*landed("mod", m))
                if m >= 2:
                    act.wait_ge(s_modused, m - 1)
                fn(WH[:, m % 2, :], raw("mod", m), ACT.Copy).then_inc(s_mhi, 1)
                if m % 2 == 1 and m >= 3:
                    mod_row_out((m - 3) // 2, (m - 3) // 2 % 2)
            mod_row_out(NB_MOD - 1, (NB_MOD - 1) % 2)
            act.wait_ge(s_lam, 1)
            fn(LT[:, 2:4], LT[:, 0:2], ACT.Exp).then_inc(s_lame, 1)

            def h_phase(h):
                l, seg = h // 2, 3 * (h % 2)
                if h != 1:
                    act.wait_ge(s_modc, {0: 1, 2: 1 + MOD_ATT, 3: 3 + MOD_ATT}[h])
                for dt in range(KT):
                    act.wait_ge(s_hps, 8 * h + dt + 1)
                    for s, lo in ((1, 0), (0, CTX)):
                        if h == 3 and s == 1:
                            continue
                        last = fn(F[:, dt, lo:lo + 256], PS[:, dt % 4, lo:lo + 256], ACT.Identity,
                                  bias=MODC[:, l, seg * 8 + dt, s:s + 1],
                                  scale=MODC[:, l, (seg + 1) * 8 + dt, s:s + 1])
                    last.then_inc(s_hf, 1)

            def project(l):
                t = 0 if l == 0 else NT0
                for c, tiles in projection(l):
                    split(c + 2)
                    for cols, dst in tiles:
                        act.wait_ge(s_qps, t + 1)
                        if isinstance(dst, str):
                            for kv in range(A_KV):
                                for half in range(2):
                                    last = fn(KTT[half * HD:(half + 1) * HD, kv, :],
                                              PS[kv * HD:(kv + 1) * HD, tile_bank(l, t), cols], ACT.Copy)
                            last.then_inc(s_qdr, 1)
                        else:
                            fn(dst, PS[:, tile_bank(l, t), cols], ACT.Copy).then_inc(s_qdr, 1)
                        t += 1

            def attention(l):
                gs = groups[l]

                def exps(gi, b, j):
                    nk = n_keys(l, b)
                    if l == 0:
                        if j == 0:
                            act.wait_ge(s_nm, gi + 1)
                        fn(S[:, gi % 2, j, 0:nk], S[:, gi % 2, j, 0:nk], ACT.Exp, bias=NM(gi)[:, j:j + 1],
                           accum_out=SU(gi)[:, j:j + 1]).then_inc(s_exp, 1)
                    else:
                        if j == 0 and gi - 2 >= NG0:
                            act.wait_ge(s_ptp, pts_before(gi - 1))
                        act.wait_ge(s_nm, NG0 + 4 * (gi - NG0) + j + 1)
                        fn(S[:, gi % 2, j, 0:nk], PS[:, score_bank(l, 4 * gi + j), 0:nk], ACT.Exp,
                           bias=NM(gi)[:, j:j + 1], scale=SCALE, accum_out=SU(gi)[:, j:j + 1]).then_inc(s_exp, 1)

                def sinks(gi, g):
                    if l == 0 and g < 2:
                        fn(SE(gi), SD(gi), ACT.Exp).then_inc(s_sink, 1)

                for j in range(4):
                    exps(g_base[l], gs[0][0], j)
                sinks(g_base[l], gs[0][1])
                for i, (b, g) in enumerate(gs):
                    gi = g_base[l] + i
                    units = 4 if l == 0 else 2
                    if l == 1 and i + 1 < len(gs):
                        exps(gi + 1, gs[i + 1][0], 0)
                    if l == 0 and i % 2 == 0 and i >= 2:
                        mod_row_out(NB_MOD + i // 2 - 1, 7)
                    for j in range(4):
                        if j < units:
                            n = pts_before(gi) + j
                            act.wait_ge(s_ptp, n + 1)
                            nk = n_keys(l, b)
                            fn(PT[:, n % 2, 0:nk], PS[:, 2 + n % 2, 0:nk], ACT.Copy).then_inc(s_ptc, 1)
                        if i + 1 < len(gs) and j >= 1:
                            exps(gi + 1, gs[i + 1][0], j - 1 if l == 0 else j)
                        if i + 1 < len(gs) and l == 0 and j == 3:
                            exps(gi + 1, gs[i + 1][0], 3)
                    if i + 1 < len(gs):
                        sinks(gi + 1, gs[i + 1][1])
                    if i == NG0 - 1:
                        mod_row_out(NB_MOD + i // 2, 7)
                    if g == 3:
                        if l == 1:
                            act.wait_ge(s_ssq, i // 4 + 1)
                            fn(SS2, SS, ACT.Sqrt).then_inc(s_ssr, 1)
                        n = i // 4 + (0 if l == 0 else 4)
                        act.wait_ge(s_otp, n + 1)
                        for half in range(2):
                            fn(HH[:, half * 4:half * 4 + 4, b * P:(b + 1) * P],
                               PS[:, turn_banks[half], :].rearrange("p (j q) -> p j q", j=4), ACT.Copy).then_inc(s_oth, 1)

            def gates(p):
                n = (0, 4, 8, 10)[p]
                for s in ((0, 1) if p < 2 else (1,)):
                    for half in range(2):
                        act.wait_ge(s_gps, n + 1)
                        fn(GATE[:, s, half * 512:(half + 1) * 512], PS[:, 4 + s * 2 + half, :], ACT.Copy)\
                            .then_inc(s_gate, 1)
                        n += 1

            def norm(p):
                n0 = NB_MOD + MOD_ATT + p * MOD_GAP
                if p < 2:
                    mod_row_out(n0, n0 % 2)
                act.wait_ge(s_var, p + 1)
                n = len(ln_blocks(p))
                fn(SQ[:, 0:n], SV[:, 0:n], ACT.Sqrt).then_inc(s_std, 1)
                act.wait_ge(s_rs, p + 1)
                for i, b in enumerate(ln_blocks(p)):
                    fn(X[:, b, :], X[:, b, :], ACT.Identity, bias=NMR[:, i:i + 1], scale=RS[:, i:i + 1])\
                        .then_inc(s_xh, 1)
                if p < 2:
                    mod_row_out(n0 + 1, (n0 + 1) % 2)

            def mixer(l):
                h_phase(2 * l)
                project(l)
                attention(l)
                gates(2 * l)
                c0 = C_OUT0 if l == 0 else C_OUT1
                split(c0 + 5)
                norm(2 * l)

            split(2)
            mixer(0)
            h_phase(1)
            gates(1)
            for st in range(FT // 2):
                cg = C_UP + 2 * st
                split(cg + 2)
                for j in range(2):
                    act.wait_ge(s_up, 4 * st + j + 1)
                    if st >= 1:
                        act.wait_ge(s_mul, 2 * st - 1 + j)
                    fn(T[:, j, :], PS[:, st % 2 * 4 + j, :], ACT.Silu).then_inc(s_silg, 1)
                    if j == 0:
                        split(cg + 3)
                if st < FT // 2 - 1:
                    split(cg + 4)
            split(C_DN + 2)

            def product_hi(j):
                if j >= 2:
                    act.wait_ge(s_dn, j - 1)
                act.wait_ge(s_mul, 2 * j + 2)
                fn(GH[:, j % 2, :, :], GT[:, 2 * j:2 * j + 2, :], ACT.Copy).then_inc(s_gh, 1)

            product_hi(0)
            product_hi(1)
            for j in range(FT // 2):
                split(min(C_DN + j + 3, C_IN1 + 1))
                if j + 2 < FT // 2:
                    product_hi(j + 2)
            norm(1)
            mixer(1)
            h_phase(3)
            for i in range(2):
                act.wait_ge(s_gx, i + 1)
                fn(EV[:, 1:2], EV[:, 0:1], ACT.Exp).then_inc(s_ge, 1)
            gates(3)
            act.wait_ge(*used[C_MOE - 1])

            def gathered(half, i):
                act.wait_ge(s_gat, i * 2 + (half + 1))
                if half == 0 and not isinstance(i, int):
                    act.wait_ge(s_he, i)
                for j in range(4):
                    dt = half * 4 + j
                    last = fn(FE[:, dt, :], PS[:, 7, j * P:(j + 1) * P], ACT.Identity,
                              bias=MODC[:, 1, 24 + dt, 0:1], scale=MODC[:, 1, 32 + dt, 0:1])
                last.then_inc(s_gev, 1)

            def copy_out():
                for nh in range(2):
                    fn(Y[:, nh, :], PS[:, 4 + nh, :], ACT.Copy).then_inc(s_y, 1)

            gathered(0, 0)
            gathered(1, 0)
            act.wait_ge(s_y0, 1)
            n_items = count_load(act)
            with act.Fori(0, n_items) as i:
                for q in range(CPI):
                    act.wait_ge(s_mland[q % MRING], i * (16 * CPI // MRING) + 16 * (q // MRING + 1))
                    act.wait_ge(*item_used(q, i))
                    fn(expert_split(q)[0], expert_raw(q), ACT.Copy).then_inc(s_hi, 1)
                    if q == MSPLIT - 1:
                        act.wait_ge(s_mdn, i * (2 * NST) + 3)
                        copy_out()
                    if q == place(*GATHER[0]) + MSPLIT:
                        gathered(0, i + 1)
                    if q == place("g", 1, 1) + MSPLIT:
                        act.wait_ge(s_gtp, i + 1)
                        fn(BACK[:, :], PS[:, 7, 0:2 * P], ACT.Copy).then_inc(s_gtc, 1)
                    for st in range(NST):
                        if q == behind("silu", st):
                            act.wait_ge(s_mup, up_done(i, "g", st, 1))
                            act.wait_ge(s_mrd, i * NST + max(st, 1))
                            fn(MT[:, st % 2, :], PS[:, st % 2 * 2, :], ACT.Silu).then_inc(s_msil, 1)
                        if q == behind("turn", st):
                            act.wait_ge(s_tp, i * NST + (st + 1))
                            if st >= 2:
                                act.wait_ge(s_mdn, down_done(i, st - 2, 1))
                            else:
                                act.wait_ge(s_mdn, i * (2 * NST) + 3)
                            fn(TH[:, st % 2, :], PS[:, 6, :], ACT.Copy).then_inc(s_th, 1)
                gathered(1, i + 1)
            act.wait_ge(s_mdn, n_items * (2 * NST) + 3)
            copy_out()
            norm(3)

        @block.vector
        def _(dve):
            v = nc.vector
            done = [0]
            chain = [0]
            term = [0]

            chain_sem = [s_dve]

            def link(ins):
                ins.then_inc(chain_sem[0], 1)
                chain[0] += 1
                dve.wait_ge(chain_sem[0], term[0] + chain[0])

            def split(upto):
                for c in range(done[0], min(upto, C_MOE)):
                    dve.wait_ge(s_hi, c + 1)
                    v.tensor_tensor(WL[:, c % 2, :], raw("weight", c), WH[:, c % 2, :].bitcast(F32),
                                    ALU.subtract).then_inc(s_lo, 1)
                    done[0] = c + 1

            dve.wait_ge(s_vt, 1)
            v.tensor_copy(VT[:, :], PS[:, 7, 0:112]).then_inc(s_vtc, 1)
            dve.wait_ge(s_vtc, 1)
            dve.wait_ge(s_sth, 1)
            v.tensor_tensor(STS[:, :, 2:4], ST[:, :, :], STS[:, :, 0:2].bitcast(F32), ALU.subtract)\
                .then_inc(s_stl, 1)
            for m in range(N_MOD):
                dve.wait_ge(s_mhi, m + 1)
                v.tensor_tensor(WL[:, m % 2, :], raw("mod", m), WH[:, m % 2, :].bitcast(F32),
                                ALU.subtract).then_inc(s_mlo, 1)
            dve.wait_ge(s_small, 48)
            lp = LAMP[:, :].rearrange("p (a b c) -> p a b c", a=2, b=2)
            prod = SM[:, 240:368].rearrange("p (a c) -> p a c", a=2)
            link(v.tensor_tensor(prod, lp[:, :, 0, :], lp[:, :, 1, :], ALU.mult))
            v.reduce_sum(LT[:, 0:2], prod, AX.X).then_inc(s_lam, 1)
            link(v.tensor_scalar(SUBL[:, :], SUBL[:, :], 1.0 - LAM_INIT, None, ALU.mult))
            for l in range(DEPTH):
                for seg in (1, 4):
                    at = VT[:, l * 48 + seg * 8:l * 48 + seg * 8 + 8]
                    link(v.tensor_scalar(at, at, 1.0, None, ALU.add))
            mod_batches = [0]

            def mod_columns(n0, n1, bank):
                mod_batches[0] += 1
                dve.wait_ge(s_modcol, mod_batches[0])
                l, nb = divmod(n0, NB_MOD)
                nb, ne = nb * 4, (nb + n1 - n0) * 4
                ps = PS[:, bank, nb * 2:ne * 2].rearrange("p (n s) -> p n s", s=2)
                v.tensor_tensor(MODC[:, l, nb:ne, :], ps, VT[:, l * 48 + nb:l * 48 + ne].unsqueeze(2)
                                .to_broadcast([P, ne - nb, 2]), ALU.add).then_inc(s_modc, 1)

            mod_columns(0, NB_MOD, 2)
            dve.wait_ge(s_lame, 1)
            link(v.tensor_tensor(LAM, LT[:, 3:4], LT[:, 2:3], ALU.subtract))
            link(v.tensor_scalar(LAM, LAM, -LAM_INIT, None, ALU.add))

            def mask_biases():
                dve.wait_ge(s_bl, 16 * ROWS * ROWS)
                for b in range(2):
                    rows = BIAS[:, b, :, :].rearrange("p h (r c) -> p (h r) c", r=ROWS)
                    mask = CN[:, C_MB:C_MB + GRID_W].unsqueeze(1).to_broadcast([P, B_HEADS * ROWS, GRID_W])
                    link(v.scalar_tensor_tensor(rows, rows, 1.0 / SCALE, mask, ALU.mult, ALU.add))
            def h_phase(h):
                toks = slice(0, TOK)
                for dt in range(KT):
                    dve.wait_ge(s_hf, 8 * h + dt + 1)
                    link(v.tensor_copy(HH[:, dt, toks], F[:, dt, toks]))
                    v.tensor_tensor(HL[:, dt, toks], F[:, dt, toks], HH[:, dt, toks].bitcast(F32),
                                    ALU.subtract).then_inc(s_hr, 1)

            def rope(l, i):
                cos, sin = CN[:, C_COS:C_COS + SEQ], CN[:, C_SIN:C_SIN + SEQ]
                for n, tt, j in rope_tiles(l, i):
                    t = tt[:, j, CTX:TOK]
                    dve.wait_ge(s_rps, n + 1)
                    if n >= 1:
                        dve.wait_ge(s_rope, n)
                    link(v.tensor_tensor(OSB[:, 0:SEQ], PS[:, 6 + n % 2, 0:SEQ], sin, ALU.mult))
                    link(v.tensor_tensor(t, t, cos, ALU.mult))
                    v.tensor_tensor(t, t, OSB[:, 0:SEQ], ALU.add).then_inc(s_rope, 1)

            def attention(l):
                gs = groups[l]
                n_sink = [0]
                if l == 0:
                    dve.wait_ge(s_zero, 1)

                def front(gi, b, g):
                    nk = n_keys(l, b)
                    two = l == 0 and b >= 2
                    if l == 1:
                        for j in range(4):
                            u = 4 * gi + j
                            dve.wait_ge(s_sc, u + 1)
                            link(v.reduce_max(MX(gi)[:, j:j + 1], PS[:, score_bank(l, u), 0:nk], AX.X))
                            v.tensor_scalar(NM(gi)[:, j:j + 1], MX(gi)[:, j:j + 1], -SCALE, None, ALU.mult)\
                                .then_inc(s_nm, 1)
                        return
                    for j in range(4):
                        u = 4 * gi + j
                        dve.wait_ge(s_sc, u + 1)
                        if j == 0 and gi - 2 >= g_base[l]:
                            dve.wait_ge(s_ptp, pts_before(gi - 1))
                        mx = MX(gi)
                        if two:
                            add = CN[:, C_MA + (b - 2) * SEQ:C_MA + (b - 1) * SEQ] if g < 2 else \
                                BIAS[:, b - 2, 4 * (g - 2) + j, :]
                            v.tensor_tensor_reduce(out=S[:, gi % 2, j, CTX:TOK], in0=PS[:, u % 2, CTX:TOK], in1=add,
                                                   scale=SCALE, scalar=-3e38, op0=ALU.add, op1=ALU.max,
                                                   accum_out=mx[:, 2 * j:2 * j + 1])
                            v.tensor_tensor_reduce(out=S[:, gi % 2, j, 0:CTX], in0=PS[:, u % 2, 0:CTX],
                                                   in1=ZERO[:, 0:CTX], scale=SCALE, scalar=-3e38, op0=ALU.add,
                                                   op1=ALU.max, accum_out=mx[:, 2 * j + 1:2 * j + 2])\
                                .then_inc(s_scd, 1)
                        else:
                            v.tensor_tensor_reduce(out=S[:, gi % 2, j, 0:nk], in0=PS[:, u % 2, 0:nk],
                                                   in1=ZERO[:, 0:nk], scale=SCALE, scalar=-3e38, op0=ALU.add,
                                                   op1=ALU.max, accum_out=mx[:, j:j + 1]).then_inc(s_scd, 1)
                    dve.wait_ge(s_scd, 4 * gi + 4)
                    top = MX(gi)[:, 0:4]
                    if two:
                        link(v.reduce_max(MM(gi), MX(gi).rearrange("p (j t) -> p j t", t=2), AX.X))
                        top = MM(gi)
                    if l == 0 and g < 2:
                        link(v.tensor_tensor(MM(gi), top, SINK[:, 4 * g:4 * g + 4], ALU.max))
                        top = MM(gi)
                        link(v.tensor_tensor(SD(gi), SINK[:, 4 * g:4 * g + 4], top, ALU.subtract))
                    v.tensor_scalar(NM(gi), top, -1.0, None, ALU.mult).then_inc(s_nm, 1)

                def back(i, gi, b, g):
                    dve.wait_ge(s_exp, 4 * gi + 4)
                    if l == 0:
                        if g < 2:
                            n_sink[0] += 1
                            dve.wait_ge(s_sink, n_sink[0])
                            link(v.tensor_tensor(SU(gi), SU(gi), SE(gi), ALU.add))
                        link(v.reciprocal(RI(gi), SU(gi)))
                        dve.wait_ge(s_ops, gi + 1)
                        if g == 0 and gi >= 4:
                            dve.wait_ge(s_otp, gi // 4)
                        v.tensor_tensor(OSB[:, g * 256:(g + 1) * 256].rearrange("p (j d) -> p j d", j=4),
                                        PS[:, 4 + gi % 2, 0:256].rearrange("p (j d) -> p j d", j=4),
                                        RI(gi).unsqueeze(2).to_broadcast([P, 4, HD]), ALU.mult)\
                            .then_inc(s_osb, 1)
                    else:
                        dve.wait_ge(s_ops, gi + 1)
                        if g == 0:
                            dve.wait_ge(s_otp, 4 + i // 4)
                        r = RI(gi).rearrange("p (h i) -> p h i", i=2)
                        v.tensor_tensor(OSB[:, g * 256:(g + 1) * 256].rearrange("p (h d) -> p h d", h=2),
                                        PS[:, 4 + gi % 2, 0:256].rearrange("p (h d) -> p h d", h=2),
                                        r[:, :, 0:1].to_broadcast([P, 2, P]), ALU.mult).then_inc(s_osb, 1)
                        dve.wait_ge(s_osb, gi + 1)
                        og, tq = OSB[:, g * 256:(g + 1) * 256], TQ[:, g * 256:(g + 1) * 256]
                        link(v.tensor_tensor(tq, og, og, ALU.mult))
                        link(v.reduce_sum(SS[:, 2 * g:2 * g + 2], tq.rearrange("p (h e) -> p h e", h=2), AX.X))
                        og = og.rearrange("p (h e) -> p h e", h=2)
                        link(v.tensor_tensor(og, og, SUBL[:, :].unsqueeze(1).to_broadcast([P, 2, P]), ALU.mult))

                def combine(gi):
                    dve.wait_ge(s_exp, 4 * gi + 4)
                    link(v.reciprocal(RI(gi), SU(gi)))
                    r = RI(gi).rearrange("p (h i) -> p h i", i=2)
                    sums = SU(gi).rearrange("p (h i) -> p h i", i=2)
                    link(v.scalar_tensor_tensor(r[:, :, 1], r[:, :, 1], LAM, sums[:, :, 0], ALU.mult, ALU.mult))
                    for h in range(2):
                        p0, p1 = S[:, gi % 2, 2 * h, :], S[:, gi % 2, 2 * h + 1, :]
                        v.scalar_tensor_tensor(p0, p1, RI(gi)[:, 2 * h + 1:2 * h + 2], p0, ALU.mult, ALU.add)\
                            .then_inc(s_cmb, 1)

                front(g_base[l], *gs[0])
                for i, (b, g) in enumerate(gs):
                    gi = g_base[l] + i
                    if l == 1:
                        combine(gi)
                    if i + 1 < len(gs):
                        front(gi + 1, *gs[i + 1])
                    n = NB_MOD + (i - 3) // 2
                    if l == 0 and i % 2 == 1 and i >= 3:
                        mod_columns(n, n + 1, 6)
                    back(i, gi, b, g)
                    if i == NG0 - 1:
                        mod_columns(n + 1, n + 2, 7)
                    if g == 3:
                        dve.wait_ge(s_osb, gi + 1)
                        n = i // 4 + (0 if l == 0 else 4)
                        if l == 1:
                            ov = OSB[:, :].rearrange("p (h e) -> p h e", h=C_HEADS)
                            v.tensor_scalar(SS, SS, 1.0 / P, EPS, ALU.mult, ALU.add).then_inc(s_ssq, 1)
                            dve.wait_ge(s_ssr, i // 4 + 1)
                            link(v.reciprocal(SS, SS2))
                            v.tensor_tensor(ov, ov, SS.unsqueeze(2).to_broadcast([P, C_HEADS, P]), ALU.mult)\
                                .then_inc(s_ob, 1)
                        dve.wait_ge(s_oth, 2 * n + 2)
                        for half in range(2):
                            dst = slice(half * 4, half * 4 + 4)
                            last = v.tensor_tensor(HL[:, dst, b * P:(b + 1) * P],
                                                   PS[:, turn_banks[half], :].rearrange("p (j q) -> p j q", j=4),
                                                   HH[:, dst, b * P:(b + 1) * P].bitcast(F32), ALU.subtract)
                        last.then_inc(s_otr, 1)

            def residual(p, nh):
                bs = ln_blocks(p)
                dve.wait_ge(s_gate, (4, 8, 10, 12)[p])
                for i, b in enumerate(bs):
                    half = slice(nh * 512, (nh + 1) * 512)
                    if p == 1:
                        dve.wait_ge(s_dn, FT // 2 + nh)
                    elif p < 3:
                        dve.wait_ge(s_yps, y_before[p] + nh * len(bs) + i + 1)
                    y = ACC[:, i * 2 + nh, :] if p == 3 else PS[:, nh * 4 + b, :]
                    link(v.tensor_tensor(TMP[:, :], y, GATE[:, b // 2, half], ALU.mult))
                    v.scalar_tensor_tensor(X[:, b, half], X[:, b, half], ALPHA, TMP[:, :],
                                           ALU.mult, ALU.add).then_inc(s_yread, 1)
                    dve.wait_ge(s_yread, y_read[p] + nh * len(bs) + i + 1)
                    link(v.bn_stats(ST6[:, i, nh * 6:nh * 6 + 6], X[:, b, half]))

            def norm(p):
                bs = ln_blocks(p)
                for i, b in enumerate(bs):
                    link(v.bn_aggr(MV[:, i, :], ST6[:, i, :]))
                n = len(bs)
                v.tensor_scalar(SV[:, 0:n], MV[:, 0:n, 1], EPS, None, ALU.add).then_inc(s_var, 1)
                dve.wait_ge(s_std, p + 1)
                link(v.reciprocal(RS[:, 0:n], SQ[:, 0:n]))
                v.scalar_tensor_tensor(NMR[:, 0:n], MV[:, 0:n, 0], -1.0, RS[:, 0:n], ALU.mult, ALU.mult)\
                    .then_inc(s_rs, 1)
                dve.wait_ge(s_lnr, 32 * (p + 1))
                for i, b in enumerate(bs):
                    xb = X[:, b, :]
                    dve.wait_ge(s_xh, ln_before[p] + i + 1)
                    link(v.tensor_tensor(xb, xb, LNR[:, 0, :], ALU.mult))
                    v.tensor_tensor(xb, xb, LNR[:, 1, :], ALU.add).then_inc(s_ln, 1)
                if p < 2:
                    n0 = NB_MOD + MOD_ATT + p * MOD_GAP
                    mod_columns(n0, n0 + MOD_GAP, 3)

            def mixer(l):
                h_phase(2 * l)
                for i, (c, _) in enumerate(projection(l)):
                    split(c + 2)
                    if i >= 1:
                        rope(l, i - 1)
                    if l == 0 and i == 5:
                        mask_biases()
                dve.wait_ge(s_rope, N_ROPE0 if l == 0 else N_ROPE)
                attention(l)
                c0 = C_OUT0 if l == 0 else C_OUT1
                split(c0 + 4)
                residual(2 * l, 0)
                split(c0 + 5)
                residual(2 * l, 1)
                norm(2 * l)

            split(2)
            mixer(0)
            h_phase(1)
            for st in range(FT // 2):
                cg = C_UP + 2 * st
                split(cg + 3)
                for j in range(2):
                    if j == 1 and st < FT // 2 - 1:
                        split(cg + 4)
                    dve.wait_ge(s_silg, 2 * st + j + 1)
                    dve.wait_ge(s_up, 4 * st + 3 + j)
                    v.tensor_tensor(GT[:, 2 * st + j, :], T[:, j, :], PS[:, st % 2 * 4 + 2 + j, :],
                                    ALU.mult).then_inc(s_mul, 1)
            split(C_DN + 2)

            def product_lo(j):
                dve.wait_ge(s_gh, j + 1)
                v.tensor_tensor(GL[:, j % 2, :, :], GT[:, 2 * j:2 * j + 2, :], GH[:, j % 2, :, :].bitcast(F32),
                                ALU.subtract).then_inc(s_gl, 1)

            product_lo(0)
            product_lo(1)
            for j in range(FT // 2):
                split(min(C_DN + j + 3, C_IN1 + 1))
                if j + 2 < FT // 2:
                    product_lo(j + 2)
            residual(1, 0)
            residual(1, 1)
            norm(1)
            mixer(1)
            for i in range(2):
                dve.wait_ge(s_lg, i + 1)
                link(v.tensor_copy(LG, PS[:, i, 0:NE]))
                link(v.max(M8, LG))
                link(v.max_index(IDX[:, :], M8, LG))
                link(v.tensor_copy(IF, IDX[:, :]))
                v.tensor_tensor(EV[:, 0:1], M8[:, 1:2], M8[:, 0:1], ALU.subtract).then_inc(s_gx, 1)
                dve.wait_ge(s_ge, i + 1)
                link(v.tensor_scalar(EV[:, 2:3], EV[:, 1:2], 1.0, None, ALU.add))
                link(v.reciprocal(EV[:, 3:4], EV[:, 2:3]))
                link(v.tensor_tensor(EV[:, 4:5], EV[:, 1:2], EV[:, 3:4], ALU.mult))
                iota = CN[:, C_IOTA:C_IOTA + NE]
                link(v.tensor_scalar(OH, iota, IF[:, 0:1], None, ALU.is_equal))
                link(v.tensor_scalar(MASKS[:, i, :], iota, IF[:, 1:2], None, ALU.is_equal))
                link(v.tensor_scalar(GW[:, i, :], MASKS[:, i, :], EV[:, 4:5], None, ALU.mult))
                link(v.scalar_tensor_tensor(GW[:, i, :], OH, EV[:, 3:4], GW[:, i, :], ALU.mult, ALU.add))
                link(v.tensor_tensor(MASKS[:, i, :], MASKS[:, i, :], OH, ALU.add))
            twice = lambda m: m.unsqueeze(3).to_broadcast([P, 2, NE, 2])
            pairs = lambda m: m.rearrange("p b (e t) -> p b e t", t=2)
            link(v.tensor_copy(pairs(GC), twice(GW)))
            v.tensor_copy(pairs(MASK2), twice(MASKS)).then_inc(s_rm, 1)
            dve.wait_ge(s_rk, 1)
            ranks = PS[:, 2, 0:16].rearrange("p (b e) -> p b e", b=2)
            for t in range(2):
                link(v.scalar_tensor_tensor(pairs(POS)[:, :, :, t], ranks, 1.0 - t * P, MASKS, ALU.add, ALU.mult))
            link(v.tensor_scalar(POS, POS, -1.0, None, ALU.add))
            v.tensor_tensor(PRES, PS[0:16, 3, 0:1], CM[0:16, M_THR:M_THR + 1], ALU.is_gt).then_inc(s_pr, 1)
            dve.wait_ge(s_ix, 1)
            link(v.tensor_copy(SR[0:16, 113:114], PS[0:16, 3, 8:9]))
            link(v.tensor_copy(TAB[:, 0:1], PS[0:1, 3, 16:17]))
            v.tensor_scalar(ISEL, CM[0:16, M_IOTA:M_IOTA + 16], SR[0:16, 113:114], PRES, ALU.is_equal, ALU.mult)\
                .then_inc(s_isel, 1)
            dve.wait_ge(s_tb, 1)
            v.tensor_copy(TAB[:, 8:40], PS[0:1, 3, 24:56]).then_inc(s_tab, 1)
            link(v.memset(ACC[:, :, :], 0.0))
            v.memset(BACK[:, :], 0.0).then_inc(s_ini, 1)
            v.memset(SM[:, 244:245], 0.0).then_inc(s_mrd, 1)
            v.memset(SM[:, 245:246], 0.0).then_inc(s_mdn, 3)
            n_items = count_load(dve)

            def select(i):
                c = dve.value_load(TAB[0:1, bass.ds(i + 8, 1)], min_val=0, max_val=2 * NE - 1)
                slots = CM[:, M_IOTA:M_IOTA + P]
                for b in range(2):
                    link(v.tensor_scalar(SELG[:, b, :], slots, POS[:, b, bass.ds(c, 1)], GC[:, b, bass.ds(c, 1)],
                                         ALU.is_equal, ALU.mult))
                link(v.tensor_scalar(SEL[:, 0, :], slots, POS[:, 0, bass.ds(c, 1)], None, ALU.is_equal))
                v.tensor_scalar(SEL[:, 1, :], slots, POS[:, 1, bass.ds(c, 1)], None, ALU.is_equal)\
                    .then_inc(s_sel, 1)

            def split_gathered(i):
                dve.wait_ge(s_gev, i * 2 + 2)
                link(v.tensor_copy(HE[:, :, :], FE[:, :, :]))
                v.tensor_tensor(LE[:, :, :], FE[:, :, :], HE[:, :, :].bitcast(F32), ALU.subtract)\
                    .then_inc(s_he, 1)

            def add_back(i, parts):
                for part in parts:
                    dve.wait_ge(s_sc2, i * 4 + (part + 1))
                    v.tensor_tensor(ACC[:, part, :], ACC[:, part, :], PS[:, 7 - part % 2, :], ALU.add)\
                        .then_inc(s_myd, 1)

            select(0)
            split_gathered(0)
            links = 4
            with dve.Fori(0, n_items) as i:
                start = chain[0]
                term[0] = i * links
                for q in range(CPI):
                    for st in range(NST):
                        if q == behind("mul", st):
                            dve.wait_ge(s_msil, i * NST + (st + 1))
                            dve.wait_ge(s_mup, up_done(i, "u", st, 1))
                            v.tensor_tensor(AF[:, st % 2, :], MT[:, st % 2, :], PS[:, st % 2 * 2 + 1, :],
                                            ALU.mult).then_inc(s_mrd, 1)
                    dve.wait_ge(s_hi, i * CPI + (C_MOE + q + 1))
                    wh, wl = expert_split(q)
                    v.tensor_tensor(wl, expert_raw(q), wh.bitcast(F32), ALU.subtract).then_inc(s_lo, 1)
                    if q == place("u", 0, 0) + MSPLIT:
                        add_back(i, (0, 1))
                    if q == behind("mul", 0):
                        add_back(i, (2, 3))
                    if q == place("g", 4, 0):
                        dve.wait_ge(s_gtp, i + 1)
                        select(i + 1)
                    for st in range(NST):
                        if q == behind("turn", st):
                            dve.wait_ge(s_th, i * NST + (st + 1))
                            v.tensor_tensor(TL[:, st % 2, :], PS[:, 6, :], TH[:, st % 2, :].bitcast(F32),
                                            ALU.subtract).then_inc(s_at, 1)
                dve.wait_ge(s_mup, up_done(i, "u", NST - 1, 1))
                split_gathered(i + 1)
                assert chain[0] - start == links, chain[0] - start
            chain_sem[0], chain[0], term[0] = s_dve2, 0, 0
            add_back(n_items, range(4))
            dve.wait_ge(s_myd, n_items * 4 + 4)
            residual(3, 0)
            residual(3, 1)
            norm(3)


INPUTS = ["x", "ctx", "vecs", "consts", "item_consts", "w_mod", "ln_g", "ln_b", "w_in_ab", "w_out_ab", "sink_a", "rpb_b",
          "w_in_c", "w_out_c", "lam_c", "subln_c", "w_ffn_up", "w_ffn_down", "w_router", "w_exp_up", "w_exp_down"]


def kernel(**inputs):
    import concourse.bacc as bacc
    from concourse.bass_utils import run_bass_kernel_spmd

    given = {k: np.ascontiguousarray(v) for k, v in inputs.items()}
    given["vecs"] = np.concatenate([given["b_mod"].reshape(-1, P), given["c"].reshape(-1, P),
                                    given["c_ctx"].reshape(-1, P)], axis=0)
    given["consts"] = shape_constants()
    given["item_consts"] = item_constants()
    nc = bacc.Bacc("TRN2", target_bir_lowering=False, num_devices=1)
    arrays, args = {}, []
    for name in INPUTS:
        a = given[name]
        arrays["in_" + name] = a
        args.append(nc.dram_tensor("in_" + name, a.shape, mybir.dt.from_np(a.dtype), kind="ExternalInput").ap())
    args.append(nc.dram_tensor("out_0", (1, SEQ, D), F32, kind="ExternalOutput").ap())
    trunk(nc, *args)
    return run_bass_kernel_spmd(nc, [arrays], core_ids=[0]).results[0]["out_0"]
```
